# Optimizing a Trainium2 kernel written in Bass

```python
import jax, jax.numpy as jnp
from jax import lax
import numpy as np

D_MODEL = 1024
BATCH = 1
SEQ = 1024
DEPTH = 1
DEC_BATCH = 8
DEC_SEQ = 4
PAST_LEN = 8192
PAGE_SIZE = 128

D_MIX = D_MODEL
D_POOL = D_MIX // 2
POOL_WINDOWS = (2, 4, 8, 16)
POOL_GROUP = D_POOL // len(POOL_WINDOWS)
POOL_STATE = max(POOL_WINDOWS) - 1
D_CONV = D_MIX - D_POOL
CONV_WIDTH = 31
CONV_STATE = CONV_WIDTH - 1
D_IN = D_POOL + 2 * D_CONV
D_PLE = 256
N_KEYS = 128
N_EXPERTS = N_KEYS * N_KEYS
PEER_HEADS = 8
PEER_TOPK = 16
D_KEY = 256
D_HALF = D_KEY // 2
TOK_BLOCK = 128
EPS = 1e-6

kernel_name = 'hymba_pool_conformer_peer_decoder_step'

def rmsnorm(x, g):
    xf = x.astype(jnp.float32)
    y = xf * lax.rsqrt(jnp.mean(xf * xf, axis=-1, keepdims=True) + EPS)
    return (y * g.astype(jnp.float32)).astype(x.dtype)

def layernorm(x, g, b):
    xf = x.astype(jnp.float32)
    mu = jnp.mean(xf, axis=-1, keepdims=True)
    var = jnp.mean(jnp.square(xf - mu), axis=-1, keepdims=True)
    y = (xf - mu) * lax.rsqrt(var + EPS)
    return (y * g.astype(jnp.float32) + b.astype(jnp.float32)).astype(x.dtype)

def pool_mixer(a, prefix, pos0, w_pool, pool_scale):
    T = a.shape[1]
    full = jnp.concatenate([prefix, a], axis=1)
    c = jnp.cumsum(full.astype(jnp.float32), axis=1)
    c = jnp.pad(c, ((0, 0), (1, 0), (0, 0)))
    pos = pos0 + jnp.arange(T)
    P = POOL_STATE
    outs = []
    for g, w in enumerate(POOL_WINDOWS):
        sl = slice(g * POOL_GROUP, (g + 1) * POOL_GROUP)
        win_sum = c[:, P + 1:P + 1 + T, sl] - c[:, P + 1 - w:P + 1 - w + T, sl]
        cnt = jnp.minimum(pos + 1, w).astype(jnp.float32)[None, :, None]
        y = win_sum / cnt - a[:, :, sl].astype(jnp.float32)
        outs.append(jnp.einsum('btc,cd->btd', y.astype(a.dtype), w_pool[g]))
    y = jnp.concatenate(outs, axis=-1) * pool_scale
    return y, full[:, -POOL_STATE:]

def conv_module(z, prefix, w_dw, b_dw, ln_g, ln_b):
    val, gt = z[..., :D_CONV], z[..., D_CONV:]
    u = val * jax.nn.sigmoid(gt)
    full = jnp.concatenate([prefix, u], axis=1)
    y = lax.conv_general_dilated(full, w_dw[:, None, :], window_strides=(1,), padding='VALID',
                                 dimension_numbers=('NWC', 'WIO', 'NWC'),
                                 feature_group_count=D_CONV) + b_dw
    y = jax.nn.silu(layernorm(y, ln_g, ln_b))
    return y, full[:, -CONV_STATE:]

def peer(x, w_q, sub_keys, u_tab, v_tab):
    B, T, D = x.shape
    n = B * T
    xt = jnp.pad(x.reshape(n, D), ((0, (-n) % TOK_BLOCK), (0, 0)))
    xb = xt.reshape(-1, TOK_BLOCK, D)

    def block(xk):
        q = (xk @ w_q).reshape(TOK_BLOCK, PEER_HEADS, 2, D_HALF)
        s = jnp.einsum('thpc,hpkc->thpk', q, sub_keys).astype(jnp.float32)
        sv, si = lax.top_k(s, PEER_TOPK)
        cand = (sv[:, :, 0, :, None] + sv[:, :, 1, None, :]).reshape(TOK_BLOCK, PEER_HEADS, -1)
        cand_idx = (si[:, :, 0, :, None] * N_KEYS + si[:, :, 1, None, :]).reshape(TOK_BLOCK, PEER_HEADS, -1)
        top_s, top_j = lax.top_k(cand, PEER_TOPK)
        eidx = jnp.take_along_axis(cand_idx, top_j, axis=-1)
        gate = jax.nn.softmax(top_s, axis=-1)
        u = u_tab[eidx]
        v = v_tab[eidx]
        h = jax.nn.gelu(jnp.einsum('td,thkd->thk', xk, u).astype(jnp.float32))
        coef = (gate * h).astype(xk.dtype)
        return jnp.einsum('thk,thkd->td', coef, v)

    out = lax.map(block, xb).reshape(-1, D)[:n]
    return out.reshape(B, T, D)

def layer(h, p, pool_prefix, conv_prefix, pos0, g_mix, w_in, w_pool, pool_scale, w_dw, b_dw, ln_g, ln_b,
          w_out, g_ffn, w_q, sub_keys, u_tab, v_tab, g_ple, w_ple_gate, w_ple_proj):
    xn = rmsnorm(h, g_mix)
    z = jnp.einsum('btd,de->bte', xn, w_in)
    ya, new_pool = pool_mixer(z[..., :D_POOL], pool_prefix, pos0, w_pool, pool_scale)
    yb, new_conv = conv_module(z[..., D_POOL:], conv_prefix, w_dw, b_dw, ln_g, ln_b)
    h = h + jnp.einsum('btc,cd->btd', jnp.concatenate([ya, yb], axis=-1), w_out)
    h = h + peer(rmsnorm(h, g_ffn), w_q, sub_keys, u_tab, v_tab)
    gate = jax.nn.sigmoid(jnp.einsum('btd,de->bte', rmsnorm(h, g_ple), w_ple_gate))
    h = h + jnp.einsum('btp,pd->btd', p, w_ple_proj) * gate
    return h, new_pool, new_conv

def setup_inputs(seed: int = 0) -> dict:
    key = jax.random.key(seed)
    ks = jax.random.split(key, 32)
    nrm = lambda k, shape, s: jax.random.normal(k, shape, jnp.float32) * s
    gain = lambda k, shape: 1.0 + 0.05 * jax.random.normal(k, shape, jnp.float32)
    return {
        'x_prompt': nrm(ks[0], (BATCH, SEQ, D_MODEL), 1.0),
        'x_sample': nrm(ks[1], (DEC_BATCH, DEC_SEQ, D_MODEL), 1.0),
        'state_pool': nrm(ks[2], (DEPTH, DEC_BATCH, POOL_STATE, D_POOL), 1.0),
        'state_conv': nrm(ks[3], (DEPTH, DEC_BATCH, CONV_STATE, D_CONV), 0.5),
        'p_prompt': nrm(ks[4], (DEPTH, BATCH, SEQ, D_PLE), 1.0),
        'p_sample': nrm(ks[5], (DEPTH, DEC_BATCH, DEC_SEQ, D_PLE), 1.0),
        'g_mix': gain(ks[6], (DEPTH, D_MODEL)),
        'w_in': nrm(ks[7], (DEPTH, D_MODEL, D_IN), D_MODEL ** -0.5),
        'w_pool': nrm(ks[8], (DEPTH, len(POOL_WINDOWS), POOL_GROUP, POOL_GROUP), POOL_GROUP ** -0.5),
        'pool_scale': gain(ks[9], (DEPTH, D_POOL)),
        'w_dw': nrm(ks[10], (DEPTH, CONV_WIDTH, D_CONV), CONV_WIDTH ** -0.5),
        'b_dw': nrm(ks[11], (DEPTH, D_CONV), 0.02),
        'ln_g': gain(ks[12], (DEPTH, D_CONV)),
        'ln_b': nrm(ks[13], (DEPTH, D_CONV), 0.02),
        'w_out': nrm(ks[14], (DEPTH, D_MIX, D_MODEL), D_MIX ** -0.5),
        'g_ffn': gain(ks[15], (DEPTH, D_MODEL)),
        'w_q': nrm(ks[16], (DEPTH, D_MODEL, PEER_HEADS * D_KEY), D_MODEL ** -0.5),
        'sub_keys': nrm(ks[17], (DEPTH, PEER_HEADS, 2, N_KEYS, D_HALF), D_HALF ** -0.5),
        'u_tab': nrm(ks[18], (DEPTH, N_EXPERTS, D_MODEL), D_MODEL ** -0.5),
        'v_tab': nrm(ks[19], (DEPTH, N_EXPERTS, D_MODEL), 0.5),
        'g_ple': gain(ks[20], (DEPTH, D_MODEL)),
        'w_ple_gate': nrm(ks[21], (DEPTH, D_MODEL, D_MODEL), D_MODEL ** -0.5),
        'w_ple_proj': nrm(ks[22], (DEPTH, D_PLE, D_MODEL), D_PLE ** -0.5),
        'g_final': gain(ks[23], (D_MODEL,)),
    }

def reference(x_prompt, x_sample, state_pool, state_conv, p_prompt, p_sample, g_mix, w_in, w_pool, pool_scale,
              w_dw, b_dw, ln_g, ln_b, w_out, g_ffn, w_q, sub_keys, u_tab, v_tab, g_ple, w_ple_gate, w_ple_proj,
              g_final):
    hp, hs = x_prompt, x_sample
    B = x_prompt.shape[0]
    pool_p, conv_p, pool_s, conv_s = [], [], [], []
    for i in range(DEPTH):
        params = (g_mix[i], w_in[i], w_pool[i], pool_scale[i], w_dw[i], b_dw[i], ln_g[i], ln_b[i], w_out[i],
                  g_ffn[i], w_q[i], sub_keys[i], u_tab[i], v_tab[i], g_ple[i], w_ple_gate[i], w_ple_proj[i])
        zp_pool = jnp.zeros((B, POOL_STATE, D_POOL), x_prompt.dtype)
        zp_conv = jnp.zeros((B, CONV_STATE, D_CONV), x_prompt.dtype)
        hp, npool, nconv = layer(hp, p_prompt[i], zp_pool, zp_conv, 0, *params)
        pool_p.append(npool)
        conv_p.append(nconv)
        hs, spool, sconv = layer(hs, p_sample[i], state_pool[i], state_conv[i], PAST_LEN, *params)
        pool_s.append(spool)
        conv_s.append(sconv)
    y_prompt = rmsnorm(hp, g_final)
    y_sample = rmsnorm(hs, g_final)
    return (y_prompt, y_sample, jnp.stack(pool_p), jnp.stack(conv_p), jnp.stack(pool_s), jnp.stack(conv_s))


_drawn_inputs = setup_inputs


def setup_inputs(seed=0):
    import zlib

    import numpy as np

    out = dict(_drawn_inputs(seed))
    spreads = {}
    factors = {'ln_b': 3.036, 'g_ple': 7.688}
    for name, (base, spread) in spreads.items():
        noise = np.random.default_rng([zlib.crc32(name.encode()), seed]).standard_normal(out[name].shape)
        drawn = base * np.exp(spread * noise) if base else spread * noise
        out[name] = __import__('jax').numpy.asarray(drawn.astype(out[name].dtype))
    for name, factor in factors.items():
        out[name] = (out[name] * factor).astype(out[name].dtype)
    return out
```

```python
from contextlib import ExitStack

import concourse.bass as bass
from concourse import mybir

ALU = mybir.AluOpType
ACT = mybir.ActivationFunctionType
AX_X = mybir.AxisListType.X
F32 = mybir.dt.float32
F32R = mybir.dt.float32r
U32 = mybir.dt.uint32

P = 128
D = 1024
DC = D // P
SEQ = 1024
DEC_B, DEC_S = 8, 4
TS = DEC_B * DEC_S
T = SEQ + TS
NTH = 3
TH = T // NTH
NT = SEQ // P + 1
LAST = SEQ - 2 * TH
D_HALF_MIX = 512
MC = D_HALF_MIX // P
WINDOWS = (2, 4, 8, 16)
POOL_PRE = max(WINDOWS) - 1
TAPS = 31
CONV_PRE = TAPS - 1
D_PLE = 256
HEADS = 8
TOPK = 16
NKEYS = 128
EPS = 1e-6
NEG = -3.0e38
GROUP = 4
SUPER = 4
BLOCK_T = 32

VEC = {"g_mix": 0, "g_ffn": 8, "g_ple": 16, "g_final": 24, "pool_scale": 32, "b_dw": 36, "ln_g": 40, "ln_b": 44}
NVEC = 48


class Chain:

    def __init__(self, eng, sem):
        self.eng, self.sem, self.n = eng, sem, 0

    def restart(self):
        self.eng.sem_clear(self.sem)
        self.n = 0

    def step(self, ins):
        self.n += 1
        ins.then_inc(self.sem, 1)
        self.eng.wait_ge(self.sem, self.n)


ENDED = []


class Phase:

    def __init__(self, nc, name):
        self.nc, self.name, self.ctx = nc, name, ExitStack()

    def __enter__(self):
        self.ctx.__enter__()
        return self

    def __exit__(self, *a):
        return self.ctx.__exit__(*a)

    def sb(self, name, shape, dt=F32):
        return self.ctx.enter_context(self.nc.sbuf_tensor(f"{self.name}_{name}", shape, dt))

    def ps(self, name, shape):
        return self.ctx.enter_context(self.nc.psum_tensor(f"{self.name}_{name}", shape, F32))

    def sem(self, name):
        s = self.ctx.enter_context(self.nc.semaphore(f"{self.name}_{name}"))
        ENDED.append(s)
        return s

    def sems(self, name, n):
        return [self.sem(f"{name}{i}") for i in range(n)]

    def block(self):
        return self.ctx.enter_context(self.nc.Block())


def start_free(eng, sems):
    for s in sems:
        eng.sem_inc(s, 1)


def thirds(ap):
    return ap.rearrange("p (a b) -> p a b", a=NTH)


def flat(ap):
    return ap.rearrange("p a b -> p (a b)")


def flat4(ap):
    return ap.rearrange("p a b c -> p (a b) c")


def load_inputs(nc, io, M):
    with Phase(nc, "ld") as ph:
        xin = [ph.sb(f"xin{b}", [P, D]) for b in range(2)]
        xlast = ph.sb("xlast", [TS, D])
        vecs = ph.sb("vecs", [NVEC, P])
        taps = ph.sb("taps", [TAPS, D_HALF_MIX])
        spool = ph.sb("spool", [DEC_B * POOL_PRE, D_HALF_MIX])
        sconv = ph.sb("sconv", [DEC_B * CONV_PRE // 2, 2, D_HALF_MIX])
        turned = [ph.ps(f"turned{b}", [P, DC, P]) for b in range(2)]
        small = [ph.ps(f"small{b}", [P, 512]) for b in range(2)]
        x_in = ph.sems("x_in", 2)
        x_turned = ph.sems("x_turned", 2)
        x_out = ph.sems("x_out", 2)
        xlast_in, small_in = ph.sem("xlast_in"), ph.sem("small_in")
        const0, consts = ph.sem("const0"), ph.sem("consts")
        small_turned, small_out = ph.sem("small_turned"), ph.sem("small_out")
        block = ph.block()
        xp = io["x_prompt"][0].rearrange("(n p) d -> n p d", p=P)

        @block.sync
        def _(sp):
            with sp.Fori(0, SEQ // P // 2) as n:
                for b in range(2):
                    sp.wait_ge(x_out[b], n + 1)
                    sp.dma_start(xin[b][:, :], xp[bass.ds(2 * n + b, 1), :, :].rearrange("a p d -> p (a d)")).then_inc(x_in[b], 16)
            sp.dma_start(xlast[:, :], io["x_sample"].rearrange("b s d -> (b s) d")).then_inc(xlast_in, 16)

        @block.gpsimd
        def _(pool):
            nc.gpsimd.memset(M.ident[:, :], 0.0).then_inc(const0, 1)
            pool.wait_ge(const0, 1)
            nc.gpsimd.affine_select(out=M.ident[:, :], in_=M.ident[:, :], compare_op=ALU.not_equal, fill=1.0,
                                    base=0, pattern=[[-1, P]], channel_multiplier=1).then_inc(consts, 1)
            nc.gpsimd.memset(M.mean_d[:, :], 1.0 / D).then_inc(consts, 1)
            nc.gpsimd.memset(M.mean_c[:, :], 1.0 / D_HALF_MIX).then_inc(consts, 1)
            nc.gpsimd.iota(M.iota[:, :], [[1, P]], base=0, channel_multiplier=0,
                           allow_small_or_imprecise_dtypes=True).then_inc(consts, 1)

        @block.scalar
        def _(act):
            for name, row in VEC.items():
                src = io[name] if name == "g_final" else io[name][0]
                k = src.shape[0] // P
                act.dma_start(vecs[row:row + k, :], src.rearrange("(c p) -> c p", p=P)).then_inc(small_in, 16)
            act.dma_start(taps[:, :], io["w_dw"][0]).then_inc(small_in, 16)
            act.dma_start(spool[:, :], io["state_pool"][0].rearrange("b s c -> (b s) c")).then_inc(small_in, 16)
            for h in range(2):
                act.dma_start(sconv[:, h, :], io["state_conv"][0].rearrange("b s c -> (b s) c")[
                    h * 120:(h + 1) * 120, :]).then_inc(small_in, 16)
            with act.Fori(0, SEQ // P // 2) as n:
                for b in range(2):
                    act.wait_ge(x_turned[b], n + 1)
                    act.nop()
                    nc.scalar.copy(M.hT[:, :, bass.ds(n * 2 * P + b * P, P)], turned[b][:, :, :]).then_inc(x_out[b], 1)

        @block.tensor
        def _(pe):
            pe.wait_ge(consts, 4)
            start_free(pe, x_out)
            with pe.Fori(0, SEQ // P // 2) as n:
                for b in range(2):
                    pe.wait_ge(x_in[b], 16 * n + 16)
                    pe.wait_ge(x_out[b], n + 1)
                    for c in range(DC):
                        last = nc.tensor.transpose(turned[b][:, c, :], xin[b][:, c * P:(c + 1) * P], M.ident[:, :])
                    last.then_inc(x_turned[b], 1)
            pe.wait_ge(xlast_in, 16)
            pe.wait_ge(x_out[0], 1 + SEQ // P // 2)
            for c in range(DC):
                last = nc.tensor.transpose(turned[0][:, c, 0:TS], xlast[:, c * P:(c + 1) * P], M.ident[0:TS, 0:TS])
            last.then_inc(small_turned, 1)
            pe.wait_ge(small_in, 16 * (len(VEC) + 4))
            nc.tensor.transpose(small[0][:, 0:NVEC], vecs[:, :], M.ident[0:NVEC, 0:NVEC])
            for c in range(MC):
                last = nc.tensor.transpose(small[0][:, 64 + 32 * c:64 + 32 * c + TAPS], taps[:, c * P:(c + 1) * P],
                                           M.ident[0:TAPS, 0:TAPS])
            last.then_inc(small_turned, 1)
            n_pool = DEC_B * POOL_PRE
            for c in range(MC):
                last = nc.tensor.transpose(small[1][:, n_pool * c:n_pool * (c + 1)], spool[:, c * P:(c + 1) * P],
                                           M.ident[0:n_pool, 0:n_pool])
            last.then_inc(small_turned, 1)
            for h in range(2):
                pe.wait_ge(small_out, 2 + h)
                for c in range(MC):
                    last = nc.tensor.transpose(small[h][:, 120 * c:120 * (c + 1)], sconv[:, h, c * P:(c + 1) * P],
                                               M.ident[0:120, 0:120])
                last.then_inc(small_turned, 1)

        @block.vector
        def _(dve):
            dve.wait_ge(small_turned, 1)
            nc.vector.tensor_copy(M.hT[:, :, SEQ:T], turned[0][:, :, 0:TS])
            dve.wait_ge(small_turned, 2)
            nc.vector.tensor_copy(M.vec[:, :], small[0][:, 0:NVEC]).then_inc(small_out, 1)
            nc.vector.tensor_copy(M.taps[:, :, 0:TAPS], small[0][:, 64:192].rearrange("p (c k) -> p c k", c=MC)[
                :, :, 0:TAPS]).then_inc(small_out, 1)
            dve.wait_ge(small_turned, 3)
            nc.vector.tensor_copy(flat(M.pool_pre[:, :, :]), small[1][:, 0:480]).then_inc(small_out, 1)
            for h in range(2):
                dve.wait_ge(small_turned, 4 + h)
                nc.vector.tensor_copy(M.conv_pre[:, :, 120 * h:120 * (h + 1)],
                                      small[h][:, 0:480].rearrange("p (c k) -> p c k", c=MC))
            dve.wait_ge(small_out, 3)
            nc.vector.tensor_copy(M.taps[:, :, TAPS:TAPS + 1], M.vec[:, VEC["b_dw"]:VEC["b_dw"] + MC].rearrange(
                "p (c k) -> p c k", k=1))


def normalise(nc, M, name, gain, hi=None, lo=None, plain=None):
    with Phase(nc, name) as ph:
        sq = [ph.sb(f"sq{b}", [P, T]) for b in range(2)]
        ms = ph.sb("ms", [P, T])
        inv = ph.sb("inv", [P, T])
        rstd = ph.sb("rstd", [P, T])
        mean = ph.ps("mean", [P, NTH, 512])
        squared, summed = ph.sem("squared"), ph.sem("summed")
        inverted, rooted = ph.sem("inverted"), ph.sem("rooted")
        scaled, rounded, split = ph.sem("scaled"), ph.sem("rounded"), ph.sem("split")
        order = ph.sem("order")
        block = ph.block()

        @block.scalar
        def _(act):
            for c in range(DC):
                if c >= 2:
                    act.wait_ge(summed, c - 1)
                nc.scalar.activation(sq[c % 2][:, :], M.hT[:, c, :], ACT.Square).then_inc(squared, 1)
            act.wait_ge(inverted, 1)
            nc.scalar.activation(rstd[:, :], inv[:, :], ACT.Sqrt).then_inc(rooted, 1)
            if hi is not None:
                for c in range(DC):
                    act.wait_ge(scaled, c + 1)
                    nc.scalar.copy(hi[:, c, :], sq[c % 2][:, :]).then_inc(rounded, 1)

        @block.tensor
        def _(pe):
            for c in range(DC):
                pe.wait_ge(squared, c + 1)
                for th in range(NTH):
                    last = nc.tensor.matmul(mean[:, th, 0:TH], M.mean_d[:, :], sq[c % 2][:, th * TH:(th + 1) * TH],
                                            start=(c == 0), stop=(c == DC - 1))
                last.then_inc(summed, 1)

        @block.vector
        def _(dve):
            chain = Chain(dve, order)
            dve.wait_ge(summed, DC)
            chain.step(nc.vector.tensor_scalar(thirds(ms[:, :]), mean[:, :, 0:TH], EPS, None, ALU.add))
            nc.vector.reciprocal(inv[:, :], ms[:, :]).then_inc(inverted, 1)
            dve.wait_ge(rooted, 1)

            def subtract(c):
                dve.wait_ge(rounded, c + 1)
                nc.vector.tensor_tensor(lo[:, c, :], sq[c % 2][:, :], hi[:, c, :].bitcast(F32),
                                        ALU.subtract).then_inc(split, 1)

            for c in range(DC):
                if hi is not None and c >= 2:
                    subtract(c - 2)
                    dve.wait_ge(split, c - 1)
                out = sq[c % 2][:, :] if hi is not None else plain[:, c, :]
                nc.vector.scalar_tensor_tensor(out=out, in0=M.hT[:, c, :], scalar=M.vec[:, gain + c:gain + c + 1],
                                               in1=rstd[:, :], op0=ALU.mult, op1=ALU.mult).then_inc(scaled, 1)
            if hi is not None:
                subtract(DC - 2)
                subtract(DC - 1)


def three_pass(nc, out, w_hi, w_lo, x_hi, x_lo, th, first=True, final=True):
    cols = slice(th * TH, (th + 1) * TH)
    for c in range(DC):
        nc.tensor.matmul(out, w_hi[:, c, :], x_hi[:, c, cols], start=(first and c == 0), stop=False)
        nc.tensor.matmul(out, w_hi[:, c, :], x_lo[:, c, cols], start=False, stop=False)
        last = nc.tensor.matmul(out, w_lo[:, c, :], x_hi[:, c, cols], start=False, stop=(final and c == DC - 1))
    return last


def mixer(nc, io, M):
    with Phase(nc, "mx") as ph:
        raw = [ph.sb(f"raw{k}", [P, DC, P]) for k in range(2)]
        w_hi = [ph.sb(f"whi{k}", [P, DC, P], F32R) for k in range(2)]
        w_lo = [ph.sb(f"wlo{k}", [P, DC, P], F32R) for k in range(2)]
        pfull = ph.sb("pfull", [P, MC, POOL_PRE + SEQ])
        pfull_s = ph.sb("pfulls", [P, MC, DEC_B, POOL_PRE + DEC_S])
        ufull = ph.sb("ufull", [P, CONV_PRE + SEQ])
        ufull_s = ph.sb("ufulls", [P, DEC_B, CONV_PRE + DEC_S])
        tap = ph.sb("tap", [P, TAPS + 1])
        sig = ph.sb("sig", [P, T])
        conv = ph.sb("conv", [P, T])
        count = ph.sb("count", [P, 16])
        part_s = ph.sb("parts", [P, 2, DEC_B, POOL_PRE + DEC_S])
        val, gate = ph.ps("val", [P, NTH, 512]), ph.ps("gate", [P, NTH, 512])
        pool_ps = ph.ps("pool", [P, 2, 512])
        w_in = ph.sems("w_in", 2)
        w_round = ph.sems("w_round", 2)
        w_split = ph.sems("w_split", 2)
        w_used = ph.sems("w_used", 2)
        sigmoid, gated, conved, moved = ph.sem("sigmoid"), ph.sem("gated"), ph.sem("conved"), ph.sem("moved")
        saved = ph.sem("saved")
        third_done, third_out = ph.sem("third_done"), ph.sem("third_out")
        order, order_s = ph.sem("order"), ph.sem("order_s")
        state_turned, state_copied, state_out = ph.sem("state_turned"), ph.sem("state_copied"), ph.sem("state_out")
        pool_order = ph.sem("pool_order")
        pooled = ph.sem("pooled")
        block = ph.block()
        w_cols = io["w_in"][0].rearrange("(c p) e -> p c e", p=P)

        @block.sync
        def _(sp):
            start_free(sp, w_split)
            with sp.Fori(0, MC) as c:
                for k in range(2):
                    sp.wait_ge(w_split[k], c + 1)
                    sp.dma_start(raw[k][:, :, :], w_cols[:, :, bass.ds(D_HALF_MIX * (1 + k) + c * P, P)]).then_inc(w_in[k], 16)
            for g in range(MC):
                k = g % 2
                sp.wait_ge(w_split[k], MC + g // 2 + 1)
                sp.dma_start(raw[k][:, :, :], w_cols[:, :, g * P:(g + 1) * P]).then_inc(w_in[k], 16)

        @block.gpsimd
        def _(pool):
            nc.gpsimd.memset(ufull[:, 0:CONV_PRE], 0.0).then_inc(pool_order, 1)
            nc.gpsimd.memset(pfull[:, :, 0:POOL_PRE], 0.0).then_inc(pool_order, 1)

            def split_weights(k, loaded, rounded):
                pool.wait_ge(w_in[k], loaded)
                pool.sem_inc(M.pool_passed, 1)
                nc.gpsimd.tensor_copy(w_hi[k][:, :, :], raw[k][:, :, :]).then_inc(w_round[k], 1)
                pool.wait_ge(w_round[k], rounded)
                nc.gpsimd.tensor_tensor(flat(w_lo[k][:, :, :]), flat(raw[k][:, :, :]),
                                        flat(w_hi[k][:, :, :]).bitcast(F32), ALU.subtract).then_inc(w_split[k], 1)

            start_free(pool, w_used)
            with pool.Fori(0, MC) as c:
                for k in range(2):
                    pool.wait_ge(w_used[k], c + 1)
                    split_weights(k, 16 * c + 16, c + 1)
                pool.wait_ge(gated, c + 2)
                pool.sem_inc(M.pool_passed, 1)
                nc.gpsimd.tensor_copy(M.ulast[:, bass.ds(c, 1), 0:CONV_PRE],
                                      ufull[:, SEQ:SEQ + CONV_PRE].rearrange("p (a b) -> p a b", a=1)).then_inc(saved, 1)
                nc.gpsimd.tensor_copy(
                    M.ulast[:, bass.ds(c, 1), CONV_PRE:CONV_PRE * 9].rearrange("p a (b s) -> p (a b) s", b=DEC_B),
                    ufull_s[:, :, DEC_S:DEC_S + CONV_PRE]).then_inc(saved, 1)
            for g in range(MC):
                k, uses = g % 2, MC + g // 2
                if g < 2:
                    pool.wait_ge(w_used[k], MC + 1)
                else:
                    pool.wait_ge(third_done, NTH * (g - 1))
                split_weights(k, 16 * (uses + 1), uses + 1)

        @block.scalar
        def _(act):
            with act.Fori(0, MC) as c:
                act.wait_ge(w_used[1], c + 2)
                act.wait_ge(gated, c + 1)
                nc.scalar.activation(thirds(sig[:, :]), gate[:, :, 0:TH], ACT.Sigmoid).then_inc(sigmoid, 1)
                act.wait_ge(conved, 2 * c + 2)
                act.nop()
                nc.scalar.copy(M.mix[:, bass.ds(c + MC, 1), :], conv[:, :].rearrange("p (a b) -> p a b", a=1)).then_inc(moved, 1)
            for g in range(MC):
                for th in range(NTH):
                    act.wait_ge(third_done, NTH * g + th + 1)
                    ps = pool_ps[:, th % 2, 0:TH]
                    if th < 2:
                        nc.scalar.copy(pfull[:, g, POOL_PRE + th * TH:POOL_PRE + (th + 1) * TH], ps).then_inc(third_out, 1)
                    else:
                        nc.scalar.copy(pfull[:, g, POOL_PRE + 2 * TH:POOL_PRE + SEQ], ps[:, 0:LAST]).then_inc(pooled, 1)
                        nc.scalar.copy(pfull_s[:, g, :, POOL_PRE:POOL_PRE + DEC_S],
                                       ps[:, LAST:TH].rearrange("p (b s) -> p b s", b=DEC_B)).then_inc(third_out, 1)

        @block.tensor
        def _(pe):
            with pe.Fori(0, MC) as c:
                for k, out in ((0, val), (1, gate)):
                    pe.wait_ge(w_split[k], c + 2)
                    pe.wait_ge(gated, c + 1)
                    for th in range(NTH):
                        last = three_pass(nc, out[:, th, 0:TH], w_hi[k], w_lo[k], M.x_hi, M.x_lo, th)
                    last.then_inc(w_used[k], 1)
            for g in range(MC):
                k = g % 2
                pe.wait_ge(w_split[k], MC + g // 2 + 2)
                for th in range(NTH):
                    need = NTH * g + (th - 1 if th == 2 else 0)
                    if need:
                        pe.wait_ge(third_out, need)
                    last = three_pass(nc, pool_ps[:, th % 2, 0:TH], w_hi[k], w_lo[k], M.x_hi, M.x_lo, th)
                    last.then_inc(third_done, 1)

        @block.vector
        def _(dve):
            dve.wait_ge(pool_order, 2)
            chain, chain_s = Chain(dve, order), Chain(dve, order_s)
            start_free(dve, (gated, saved, moved))
            with dve.Fori(0, MC) as c:
                chain.restart()
                chain_s.restart()
                dve.wait_ge(sigmoid, c + 1)
                dve.wait_ge(saved, 2 * c + 1)
                nc.vector.tensor_tensor(ufull[:, CONV_PRE:CONV_PRE + 2 * TH].rearrange("p (a b) -> p a b", a=2),
                                        val[:, 0:2, 0:TH], sig[:, 0:2 * TH].rearrange("p (a b) -> p a b", a=2), ALU.mult)
                nc.vector.tensor_tensor(ufull[:, CONV_PRE + 2 * TH:CONV_PRE + SEQ], val[:, 2, 0:LAST],
                                        sig[:, 2 * TH:SEQ], ALU.mult)
                nc.vector.tensor_copy(tap[:, :].rearrange("p (a b) -> p a b", a=1), M.taps[:, bass.ds(c, 1), :])
                nc.vector.tensor_copy(ufull_s[:, :, 0:CONV_PRE], M.conv_pre[:, bass.ds(c, 1), :].rearrange(
                    "p a (b s) -> p (a b) s", b=DEC_B))
                nc.vector.tensor_tensor(ufull_s[:, :, CONV_PRE:CONV_PRE + DEC_S],
                                        val[:, 2, LAST:TH].rearrange("p (b s) -> p b s", b=DEC_B),
                                        sig[:, SEQ:T].rearrange("p (b s) -> p b s", b=DEC_B), ALU.mult).then_inc(gated, 1)
                dve.wait_ge(gated, c + 2)
                dve.wait_ge(moved, c + 1)
                out_s = conv[:, SEQ:T].rearrange("p (b s) -> p b s", b=DEC_B)
                for k in range(TAPS):
                    src, src_s = ufull[:, k:k + SEQ], ufull_s[:, :, k:k + DEC_S]
                    if k == 0:
                        a = nc.vector.tensor_scalar(conv[:, 0:SEQ], src, tap[:, 0:1], tap[:, TAPS:TAPS + 1], ALU.mult, ALU.add)
                        b = nc.vector.tensor_scalar(out_s, src_s, tap[:, 0:1], tap[:, TAPS:TAPS + 1], ALU.mult, ALU.add)
                        a.then_inc(order, 1)
                        b.then_inc(order_s, 1)
                    else:
                        done, done_s = (order, order_s) if k < TAPS - 1 else (conved, conved)
                        dve.wait_ge(order, k)
                        nc.vector.scalar_tensor_tensor(out=conv[:, 0:SEQ], in0=src, scalar=tap[:, k:k + 1],
                                                       in1=conv[:, 0:SEQ], op0=ALU.mult, op1=ALU.add).then_inc(done, 1)
                        dve.wait_ge(order_s, k)
                        nc.vector.scalar_tensor_tensor(out=out_s, in0=src_s, scalar=tap[:, k:k + 1],
                                                       in1=out_s, op0=ALU.mult, op1=ALU.add).then_inc(done_s, 1)
            chain.restart()
            dve.wait_ge(moved, MC + 1)
            for g, w in enumerate(WINDOWS):
                dve.wait_ge(third_out, NTH * (g + 1))
                dve.wait_ge(pooled, g + 1)
                chain.step(nc.vector.tensor_copy(pfull_s[:, g, :, 0:POOL_PRE], M.pool_pre[:, g, :].rearrange(
                    "p (b s) -> p b s", b=DEC_B)))
                cur, cur_s = pfull[:, g, :], pfull_s[:, g]
                n, n_s, m = POOL_PRE + SEQ, POOL_PRE + DEC_S, 0
                while (1 << m) < w:
                    d = 1 << m
                    nxt = (conv, sig)[m % 2][:, 0:n - d]
                    nxt_s = part_s[:, m % 2, :, 0:n_s - d]
                    nc.vector.tensor_tensor(nxt, cur[:, d:n], cur[:, 0:n - d], ALU.add)
                    chain.step(nc.vector.tensor_tensor(nxt_s, cur_s[:, :, d:n_s], cur_s[:, :, 0:n_s - d], ALU.add))
                    cur, cur_s, n, n_s, m = nxt, nxt_s, n - d, n_s - d, m + 1
                chain.step(nc.vector.tensor_scalar(count[:, 0:16], M.iota[:, 0:16], 1.0, float(w), ALU.add, ALU.min))
                chain.step(nc.vector.reciprocal(count[:, 0:16], count[:, 0:16]))
                at = n - SEQ
                chain.step(nc.vector.tensor_tensor(count[:, 0:16], cur[:, at:at + 16], count[:, 0:16], ALU.mult))
                nc.vector.tensor_tensor(M.mix[:, g, 0:16], count[:, 0:16], pfull[:, g, POOL_PRE:POOL_PRE + 16], ALU.subtract)
                nc.vector.scalar_tensor_tensor(out=M.mix[:, g, 16:SEQ], in0=cur[:, at + 16:at + SEQ], scalar=1.0 / w,
                                               in1=pfull[:, g, POOL_PRE + 16:POOL_PRE + SEQ], op0=ALU.mult, op1=ALU.subtract)
                at = n_s - DEC_S
                chain.step(nc.vector.scalar_tensor_tensor(
                    out=M.mix[:, g, SEQ:T].rearrange("p (b s) -> p b s", b=DEC_B), in0=cur_s[:, :, at:n_s], scalar=1.0 / w,
                    in1=pfull_s[:, g, :, POOL_PRE:POOL_PRE + DEC_S], op0=ALU.mult, op1=ALU.subtract))
                nc.vector.tensor_copy(M.plast[:, g, 0:POOL_PRE], pfull[:, g, SEQ:SEQ + POOL_PRE])
                chain.step(nc.vector.tensor_copy(M.plast[:, g, POOL_PRE:POOL_PRE * 9].rearrange("p (b s) -> p b s", b=DEC_B),
                                                 pfull_s[:, g, :, DEC_S:DEC_S + POOL_PRE]))


def mixer_tail(nc, io, M):
    with Phase(nc, "mt") as ph:
        wp = ph.sb("wp", [P, MC, P])
        sq = [ph.sb(f"sq{b}", [P, T]) for b in range(2)]
        inv, rstd = ph.sb("inv", [P, T]), ph.sb("rstd", [P, T])
        prow = ph.sb("prow", [P, 2, D_HALF_MIX])
        crow = ph.sb("crow", [P, 3, D_HALF_MIX])
        mean = ph.ps("mean", [P, NTH, 512])
        ya = ph.ps("ya", [P, NTH, 512])
        rows = ph.ps("rows", [P, 2, 512])
        wp_in, rows_turned, rows_copied, rows_out = ph.sem("wp_in"), ph.sem("rows_turned"), ph.sem("rows_copied"), ph.sem("rows_out")
        ya_done, ya_out = ph.sem("ya_done"), ph.sem("ya_out")
        meaned, centred, squared, summed = ph.sem("meaned"), ph.sem("centred"), ph.sem("squared"), ph.sem("summed")
        inverted, rooted, normed, rounded = ph.sem("inverted"), ph.sem("rooted"), ph.sem("normed"), ph.sem("rounded")
        swished, pscaled = ph.sem("swished"), ph.sem("pscaled")
        order = ph.sem("order")
        block = ph.block()
        n_pool, n_conv = DEC_B * POOL_PRE, DEC_B * CONV_PRE // 2
        jobs = [(M.plast, 0, POOL_PRE, prow, 0), (M.plast, POOL_PRE, n_pool, prow, 1),
                (M.ulast, 0, CONV_PRE, crow, 0), (M.ulast, CONV_PRE, n_conv, crow, 1),
                (M.ulast, CONV_PRE + n_conv, n_conv, crow, 2)]
        cs = io["conv_state_sample"][0].rearrange("b s c -> (b s) c")
        dests = [io["pool_state_prompt"][0, 0], io["pool_state_sample"][0].rearrange("b s c -> (b s) c"),
                 io["conv_state_prompt"][0, 0], cs[0:n_conv, :], cs[n_conv:2 * n_conv, :]]

        @block.sync
        def _(sp):
            sp.dma_start(wp[:, :, :], io["w_pool"][0].rearrange("g c d -> c g d")).then_inc(wp_in, 16)
            for j, (_, _, n, row, r) in enumerate(jobs):
                sp.wait_ge(rows_copied, j + 1)
                sp.dma_start(dests[j], row[0:n, r, :]).then_inc(rows_out, 16)
            sp.wait_ge(rows_out, 16 * len(jobs))

        @block.tensor
        def _(pe):
            for c in range(MC):
                for th in range(NTH):
                    last = nc.tensor.matmul(mean[:, th, 0:TH], M.mean_c[:, :], M.mix[:, MC + c, th * TH:(th + 1) * TH],
                                            start=(c == 0), stop=(c == MC - 1))
            last.then_inc(meaned, 1)
            for j, (src, at, n, _, _) in enumerate(jobs):
                if j >= 2:
                    pe.wait_ge(rows_copied, j - 1)
                for c in range(MC):
                    last = nc.tensor.transpose(rows[0:n, j % 2, c * P:(c + 1) * P], src[:, c, at:at + n], M.ident[:, :])
                last.then_inc(rows_turned, 1)
            pe.wait_ge(wp_in, 16)
            pe.wait_ge(centred, MC)
            for c in range(MC):
                pe.wait_ge(squared, c + 1)
                for th in range(NTH):
                    last = nc.tensor.matmul(mean[:, th, 0:TH], M.mean_c[:, :], sq[c % 2][:, th * TH:(th + 1) * TH],
                                            start=(c == 0), stop=(c == MC - 1))
                last.then_inc(summed, 1)
            for g in range(MC):
                if g:
                    pe.wait_ge(ya_out, g)
                for th in range(NTH):
                    last = nc.tensor.matmul(ya[:, th, 0:TH], wp[:, g, :], M.mix[:, g, th * TH:(th + 1) * TH],
                                            start=True, stop=True)
                last.then_inc(ya_done, 1)

        @block.scalar
        def _(act):
            for c in range(MC):
                act.wait_ge(centred, c + 1)
                if c >= 2:
                    act.wait_ge(summed, c - 1)
                nc.scalar.activation(sq[c % 2][:, :], M.mix[:, MC + c, :], ACT.Square).then_inc(squared, 1)
            act.wait_ge(inverted, 1)
            nc.scalar.activation(rstd[:, :], inv[:, :], ACT.Sqrt).then_inc(rooted, 1)
            for g in range(MC):
                act.wait_ge(ya_done, g + 1)
                nc.scalar.activation(thirds(M.mix[:, g, :]), ya[:, :, 0:TH], ACT.Copy,
                                     scale=M.vec[:, VEC["pool_scale"] + g:VEC["pool_scale"] + g + 1]).then_inc(ya_out, 1)
            for c in range(MC):
                act.wait_ge(normed, c + 1)
                nc.scalar.activation(M.mix[:, MC + c, :], M.mix[:, MC + c, :], ACT.Silu,
                                     scale=M.vec[:, VEC["ln_g"] + c:VEC["ln_g"] + c + 1],
                                     bias=M.vec[:, VEC["ln_b"] + c:VEC["ln_b"] + c + 1]).then_inc(swished, 1)
            act.wait_ge(swished, MC)
            act.wait_ge(ya_out, MC)
            for c in range(DC):
                nc.scalar.copy(M.x_hi[:, c, :], M.mix[:, c, :]).then_inc(rounded, 1)

        @block.vector
        def _(dve):
            chain = Chain(dve, order)
            dve.wait_ge(meaned, 1)
            for c in range(MC):
                nc.vector.tensor_tensor(thirds(M.mix[:, MC + c, :]), thirds(M.mix[:, MC + c, :]), mean[:, :, 0:TH],
                                        ALU.subtract).then_inc(centred, 1)
            for j, (_, _, n, row, r) in enumerate(jobs):
                dve.wait_ge(rows_turned, j + 1)
                nc.vector.tensor_copy(row[0:n, r, :], rows[0:n, j % 2, :]).then_inc(rows_copied, 1)
            dve.wait_ge(summed, MC)
            chain.step(nc.vector.tensor_scalar(thirds(inv[:, :]), mean[:, :, 0:TH], EPS, None, ALU.add))
            nc.vector.reciprocal(inv[:, :], inv[:, :]).then_inc(inverted, 1)
            dve.wait_ge(rooted, 1)
            for c in range(MC):
                nc.vector.tensor_tensor(M.mix[:, MC + c, :], M.mix[:, MC + c, :], rstd[:, :], ALU.mult).then_inc(normed, 1)
            for c in range(DC):
                dve.wait_ge(rounded, c + 1)
                nc.vector.tensor_tensor(M.x_lo[:, c, :], M.mix[:, c, :], M.x_hi[:, c, :].bitcast(F32), ALU.subtract)


class WeightStream:

    def __init__(self, nc, ph, w, chunks):
        self.nc, self.pairs = nc, chunks // 2
        self.cols = w.rearrange("(c p) e -> p c e", p=P)
        self.raw = [ph.sb(f"raw{b}", [P, DC, P]) for b in range(2)]
        self.hi = [ph.sb(f"whi{b}", [P, DC, P], F32R) for b in range(2)]
        self.lo = [ph.sb(f"wlo{b}", [P, DC, P], F32R) for b in range(2)]
        self.loaded = ph.sems("w_loaded", 2)
        self.rounded = ph.sems("w_rounded", 2)
        self.split = ph.sems("w_split", 2)
        self.used = ph.sems("w_used", 2)
        self.passed = ph.sem("w_passed")

    def start(self, sp):
        start_free(sp, self.split + self.used)

    def load(self, sp, n, b):
        sp.wait_ge(self.split[b], n + 1)
        sp.dma_start(self.raw[b][:, :, :], self.cols[:, :, bass.ds(n * 2 * P + b * P, P)]).then_inc(self.loaded[b], 16)

    def halve(self, pool, n, b):
        pool.wait_ge(self.loaded[b], 16 * n + 16)
        pool.wait_ge(self.used[b], n + 1)
        pool.sem_inc(self.passed, 1)
        self.nc.gpsimd.tensor_copy(self.hi[b][:, :, :], self.raw[b][:, :, :]).then_inc(self.rounded[b], 1)
        pool.wait_ge(self.rounded[b], n + 1)
        self.nc.gpsimd.tensor_tensor(flat(self.lo[b][:, :, :]), flat(self.raw[b][:, :, :]),
                                     flat(self.hi[b][:, :, :]).bitcast(F32), ALU.subtract).then_inc(self.split[b], 1)

    def product(self, pe, n, b, out, x_hi, x_lo, third_done=None):
        pe.wait_ge(self.split[b], n + 2)
        for th in range(NTH):
            last = three_pass(self.nc, out[:, th, 0:TH], self.hi[b], self.lo[b], x_hi, x_lo, th)
            if third_done is not None and th < NTH - 1:
                last.then_inc(third_done, 1)
        last.then_inc(self.used[b], 1)


def out_projection(nc, io, M):
    with Phase(nc, "op") as ph:
        ws = WeightStream(nc, ph, io["w_out"][0], DC)
        out = [ph.ps(f"out{b}", [P, NTH, 512]) for b in range(2)]
        added = ph.sems("added", 2)
        block = ph.block()

        @block.sync
        def _(sp):
            ws.start(sp)
            with sp.Fori(0, ws.pairs) as n:
                for b in range(2):
                    ws.load(sp, n, b)

        @block.gpsimd
        def _(pool):
            with pool.Fori(0, ws.pairs) as n:
                for b in range(2):
                    ws.halve(pool, n, b)

        @block.tensor
        def _(pe):
            start_free(pe, added)
            with pe.Fori(0, ws.pairs) as n:
                for b in range(2):
                    pe.wait_ge(added[b], n + 1)
                    ws.product(pe, n, b, out[b], M.x_hi, M.x_lo)

        @block.vector
        def _(dve):
            with dve.Fori(0, ws.pairs) as n:
                for b in range(2):
                    dve.wait_ge(ws.used[b], n + 2)
                    row = M.hT[:, bass.ds(2 * n + b, 1), :].rearrange("p o (a b) -> p (o a) b", a=NTH)
                    nc.vector.tensor_tensor(row, row, out[b][:, :, 0:TH], ALU.add).then_inc(added[b], 1)


class Ranking:

    def __init__(self, nc, ph, M):
        self.nc, self.M = nc, M
        self.key_s, self.key_at = ph.sb("key_s", [P, 2, TOPK]), ph.sb("key_at", [P, 2, TOPK])
        self.cand, self.rest = ph.sb("cand", [P, TOPK, TOPK]), ph.sb("rest", [P, TOPK * TOPK])
        self.top, self.top_at = ph.sb("top", [P, TOPK]), ph.sb("top_at", [P, TOPK], U32)
        self.rank = ph.sb("rank", [P, 2, TOPK], U32)
        self.same = ph.sb("same", [P, 2, TOPK, TOPK])
        self.best, self.idx = ph.sb("best", [P, HEADS, TOPK]), ph.sb("idx", [P, 2, HEADS, TOPK])

    def rank_head(self, chain, tile, head):
        self.nc.vector.tensor_copy(self.key_s[:, :, :], flat4(self.M.sv[:, bass.ds(tile, 1), bass.ds(2 * head, 2), :]))
        chain.step(self.nc.vector.tensor_copy(self.key_at[:, :, :], flat4(self.M.si[:, bass.ds(tile, 1), bass.ds(2 * head, 2), :])))
        chain.step(self.nc.vector.tensor_tensor(
            self.cand[:, :, :], self.key_s[:, 0, :].unsqueeze(2).broadcast_to([P, TOPK, TOPK]),
            self.key_s[:, 1, :].unsqueeze(1).broadcast_to([P, TOPK, TOPK]), ALU.add))
        chain.step(self.nc.vector.max(self.top[:, 0:8], flat(self.cand[:, :, :])))
        self.nc.vector.max_index(self.top_at[:, 0:8], self.top[:, 0:8], flat(self.cand[:, :, :]))
        chain.step(self.nc.vector.match_replace(self.rest[:, :], self.top[:, 0:8], flat(self.cand[:, :, :]), NEG))
        chain.step(self.nc.vector.max(self.top[:, 8:16], self.rest[:, :]))
        chain.step(self.nc.vector.max_index(self.top_at[:, 8:16], self.top[:, 8:16], self.rest[:, :]))

    def name_head(self, chain, head):
        self.nc.vector.tensor_copy(self.best[:, bass.ds(head, 1), :], self.top[:, :].unsqueeze(1))
        self.nc.vector.tensor_scalar(self.rank[:, 0, :], self.top_at[:, :], 4, None, ALU.logical_shift_right)
        chain.step(self.nc.vector.tensor_scalar(self.rank[:, 1, :], self.top_at[:, :], TOPK - 1, None, ALU.bitwise_and))
        for w in range(2):
            last = self.nc.vector.tensor_tensor(self.same[:, w], self.M.iota[:, 0:TOPK].unsqueeze(1).broadcast_to([P, TOPK, TOPK]),
                                           self.rank[:, w, :].unsqueeze(2).broadcast_to([P, TOPK, TOPK]), ALU.is_equal)
        chain.step(last)
        for w in range(2):
            last = self.nc.vector.tensor_tensor(self.same[:, w], self.same[:, w],
                                           self.key_at[:, w, :].unsqueeze(1).broadcast_to([P, TOPK, TOPK]), ALU.mult)
        chain.step(last)
        for w in range(2):
            last = self.nc.vector.tensor_reduce(self.idx[:, w, bass.ds(head, 1), :].rearrange("p a k -> p (a k)"),
                                           self.same[:, w], AX_X, ALU.add)
        chain.step(last)


def key_scores(nc, io, M):
    with Phase(nc, "ks") as ph:
        ws = WeightStream(nc, ph, io["w_q"][0], 2 * HEADS)
        keys = ph.sb("keys", [P, 2 * HEADS, P])
        keysT = ph.sb("keysT", [P, 2 * HEADS, P])
        qT = [ph.sb(f"qT{b}", [P, T]) for b in range(2)]
        score = [ph.sb(f"score{b}", [P, NT, NKEYS]) for b in range(2)]
        rest = ph.sb("rest", [P, NKEYS])
        top = ph.sb("top", [P, NT, TOPK])
        top_at = ph.sb("top_at", [P, NT, TOPK], U32)
        q_ps = ph.ps("q", [P, NTH, 512])
        s_ps = ph.ps("s", [P, 3, 512])
        k_ps = ph.ps("k", [P, 2, 512])
        keys_in, keys_turned, keys_out = ph.sem("keys_in"), ph.sem("keys_turned"), ph.sem("keys_out")
        q_out, third_done = ph.sem("q_out"), ph.sem("third_done")
        scored = ph.sem("scored")
        score_out = ph.sem("score_out")
        picked = ph.sem("picked")
        order = ph.sem("order")
        cleared = ph.sem("cleared")
        block = ph.block()

        @block.sync
        def _(sp):
            sp.dma_start(keys[:, :, :], io["sub_keys"][0].rearrange("h s k c -> k (h s) c")).then_inc(keys_in, 16)
            ws.start(sp)
            with sp.Fori(0, ws.pairs) as n:
                for b in range(2):
                    ws.load(sp, n, b)

        @block.gpsimd
        def _(pool):
            for b in range(2):
                nc.gpsimd.memset(score[b][:, NT - 1, :], 0.0).then_inc(cleared, 1)
            with pool.Fori(0, ws.pairs) as n:
                for b in range(2):
                    ws.halve(pool, n, b)

        @block.tensor
        def _(pe):
            pe.wait_ge(keys_in, 16)
            for r in range(4):
                if r >= 2:
                    pe.wait_ge(keys_out, r - 1)
                for k in range(4):
                    last = nc.tensor.transpose(k_ps[:, r % 2, k * P:(k + 1) * P], keys[:, 4 * r + k, :], M.ident[:, :])
                last.then_inc(keys_turned, 1)
            pe.wait_ge(keys_out, 4)

            def scores(b, n_q, n_free, index):
                pe.wait_ge(q_out, n_q)
                pe.wait_ge(score_out, n_free)
                for t in range(NT):
                    rows = P if t < NT - 1 else TS
                    last = nc.tensor.matmul(s_ps[0:rows, t // 4, (t % 4) * P:(t % 4 + 1) * P], qT[b][:, t * P:t * P + rows],
                                            keysT[:, bass.ds(index, 1), :].rearrange("p a k -> p (a k)"),
                                            start=True, stop=True)
                last.then_inc(scored, 1)

            start_free(pe, (score_out,))
            with pe.Fori(0, ws.pairs) as n:
                for b in range(2):
                    ws.product(pe, n, b, q_ps, M.x_hi, M.x_lo, third_done)
                    scores(b, 6 * n + 3 * b + 3, 2 * n + b + 1, 2 * n + b)

        @block.scalar
        def _(act):
            for r in range(4):
                act.wait_ge(keys_turned, r + 1)
                nc.scalar.copy(keysT[:, 4 * r:4 * r + 4, :], k_ps[:, r % 2, :].rearrange("p (a b) -> p a b", a=4)).then_inc(keys_out, 1)
            act.wait_ge(cleared, 2)
            start_free(act, (scored, scored, picked, picked))
            with act.Fori(0, ws.pairs) as n:
                for b in range(2):
                    act.wait_ge(scored, 2 * n + b + 1)
                    for th in range(NTH):
                        if th < NTH - 1:
                            act.wait_ge(third_done, 4 * n + 2 * b + th + 1)
                        else:
                            act.wait_ge(ws.used[b], n + 2)
                        nc.scalar.copy(qT[b][:, th * TH:(th + 1) * TH], q_ps[:, th, 0:TH]).then_inc(q_out, 1)
                    act.wait_ge(scored, 2 * n + b + 3)
                    act.wait_ge(picked, 2 * n + b + 1)
                    nc.scalar.copy(score[b][:, 0:8, :].rearrange("p (a c) k -> p a c k", a=2),
                                   s_ps[:, 0:2, :].rearrange("p a (c k) -> p a c k", c=4))
                    nc.scalar.copy(score[b][0:TS, 8, :], s_ps[0:TS, 2, 0:P]).then_inc(score_out, 1)

        @block.vector
        def _(dve):
            chain = Chain(dve, order)
            with dve.Fori(0, ws.pairs) as n:
                chain.restart()
                for b in range(2):
                    dve.wait_ge(picked, 2 * n + b + 2)
                    dve.wait_ge(score_out, 2 * n + b + 2)
                    dve.sem_inc(M.dve_passed, 1)
                    for t in range(NT):
                        s = score[b][:, t, :]
                        chain.step(nc.vector.max(top[:, t, 0:8], s))
                        nc.vector.max_index(top_at[:, t, 0:8], top[:, t, 0:8], s)
                        chain.step(nc.vector.match_replace(rest[:, :], top[:, t, 0:8], s, NEG))
                        chain.step(nc.vector.max(top[:, t, 8:16], rest[:, :]))
                        chain.step(nc.vector.max_index(top_at[:, t, 8:16], top[:, t, 8:16], rest[:, :]))
                    nc.vector.tensor_copy(M.sv[:, :, bass.ds(2 * n + b, 1), :].rearrange("p t a k -> p t (a k)"), top[:, :, :])
                    nc.vector.tensor_copy(M.si[:, :, bass.ds(2 * n + b, 1), :].rearrange("p t a k -> p t (a k)"),
                                          top_at[:, :, :]).then_inc(picked, 1)
                dve.wait_ge(picked, 2 * n + 4)
                dve.sem_inc(M.dve_passed, 1)
                M.ranking.rank_head(chain, 0, n)
                M.ranking.name_head(chain, n)


CHUNKS_A_TILE = NKEYS // (SEQ // P)
GROUPS_A_CHUNK = 2
GROUPS_A_TILE = GROUPS_A_CHUNK * CHUNKS_A_TILE
BLOCKS_A_TILE = P // BLOCK_T
SLOTS = 4
N_TILES = SEQ // P
BLOCKS = T // BLOCK_T


def hidden_and_weights(nc, io, M):
    with Phase(nc, "hw") as ph:
        raw = [ph.sb(f"raw{b}", [P, D]) for b in range(2)]
        u_hi = [ph.sb(f"uhi{b}", [P, DC, P], F32R) for b in range(2)]
        u_lo = [ph.sb(f"ulo{b}", [P, DC, P], F32R) for b in range(2)]
        hid = [ph.sb(f"hid{b}", [P, T]) for b in range(2)]
        weight = [ph.sb(f"wt{b}", [P, NKEYS // SUPER, BLOCK_T * SUPER]) for b in range(2)]
        one_j = ph.sb("one_j", [P, SLOTS, GROUP, NKEYS], F32R)
        one_i = ph.sb("one_i", [P, SLOTS, GROUP, 2, NKEYS], F32R)
        picks = ph.sb("picks", [P, 4, P])
        gate_hi = ph.sb("gate_hi", [P, P], F32R)
        curs = [ph.sb(f"cur{b}", [P, 4, 2 * GROUP]) for b in range(2)]
        best, idx = M.ranking.best, M.ranking.idx
        prob, expo = ph.sb("prob", [P, HEADS, TOPK]), ph.sb("expo", [P, HEADS, TOPK])
        total = ph.sb("total", [P, HEADS])

        hid_ps = ph.ps("hid", [P, NTH, 512])
        turned = ph.ps("turned", [P, DC, P])
        w_ps = [ph.ps(f"w{b}", [P, GROUP // 2, 2, NKEYS]) for b in range(2)]
        pick_ps = ph.ps("pick", [P, 4, P])

        u_in, u_turned = ph.sems("u_in", 2), ph.sem("u_turned")
        u_round, u_split = ph.sem("u_round"), ph.sem("u_split")
        third_done, third_out = ph.sem("third_done"), ph.sem("third_out")
        hid_stored, hid_free = ph.sems("hid_stored", 2), ph.sems("hid_free", 2)
        one_made = ph.sems("one_made", SLOTS)
        w_done, hi_out, w_out, w_stored = ph.sems("w_done", 2), ph.sems("hi_out", 2), ph.sems("w_out", 2), ph.sems("w_stored", 2)
        shifted, exped, probed, picks_turned = ph.sem("shifted"), ph.sem("exped"), ph.sem("probed"), ph.sem("picks_turned")
        order = ph.sem("order")
        block = ph.block()
        u_rows = io["u_tab"][0].rearrange("(n p) d -> n p d", p=P)

        def block_view(group, bank):
            t0 = (group % 8 * GROUP + bank * (GROUP // 2)) * SUPER
            return weight[group // 8 % 2][:, :, t0:t0 + GROUP // 2 * SUPER].rearrange("p s (t i) -> p t s i", i=SUPER)

        @block.sync
        def _(sp):
            start_free(sp, (u_turned, u_turned))
            with sp.Fori(0, NKEYS // 2) as n:
                for b in range(2):
                    sp.wait_ge(u_turned, 2 * n + b + 1)
                    sp.dma_start(raw[b][:, :], u_rows[bass.ds(2 * n + b, 1), :, :].rearrange("a p d -> p (a d)")).then_inc(u_in[b], 16)
            sp.wait_ge(u_turned, NKEYS + 1)
            sp.dma_start(raw[0][:, :], u_rows[0]).then_inc(u_in[0], 16)

        @block.gpsimd
        def _(pool):
            with pool.Fori(0, NKEYS // 2) as n:
                for b in range(2):
                    pool.wait_ge(third_out, NTH * (2 * n + b + 2))
                    pool.dma_start(M.hidden[bass.ds(2 * n + b, 1), :, :].rearrange("a p t -> p (a t)"),
                                   hid[b][:, :]).then_inc(hid_stored[b], 16)
                    pool.wait_ge(hid_stored[b], 16 * n + 16)
                    pool.sem_inc(hid_free[b], 1)
            for b in range(2):
                pool.wait_ge(w_stored[b], 16 * ((BLOCKS + 1 - b) // 2 + 1))

        @block.scalar
        def _(act):
            def round_u(b, n_turned):
                act.wait_ge(u_turned, n_turned + 2)
                nc.scalar.copy(u_hi[b][:, :, :], turned[:, :, :]).then_inc(u_round, 1)

            def hi_to_block(group, n):
                blk = group // 8
                if group % 8 == 0:
                    act.wait_ge(w_stored[blk % 2], 16 * (n * (BLOCKS_A_TILE // 2) + blk // 2 + 1))
                for bank in range(2):
                    act.wait_ge(w_done[bank], n * GROUPS_A_TILE + group + SLOTS + 1)
                    half = w_ps[bank][:, :, 0, :].rearrange("p t (s i) -> p t s i", i=SUPER)
                    nc.scalar.copy(block_view(group, bank), half).then_inc(hi_out[bank], 1)

            def store_block(blk, n):
                for bank in range(2):
                    act.wait_ge(w_out[bank], n * GROUPS_A_TILE + 8 * blk + 9)
                act.dma_start(M.weights[:, :, bass.ds((n * BLOCKS_A_TILE + blk) * (BLOCK_T * SUPER), BLOCK_T * SUPER)].rearrange(
                    "s j t -> j s t"), weight[blk % 2][:, :, :]).then_inc(w_stored[blk % 2], 16)

            def exponentials(n_shifted):
                act.wait_ge(shifted, n_shifted)
                nc.scalar.activation(expo[:, :, :], prob[:, :, :], ACT.Exp).then_inc(exped, 1)

            start_free(act, (third_out,) * NTH)
            start_free(act, hid_free + w_out)
            for s in w_stored:
                act.sem_inc(s, 16)
            round_u(0, 1)
            exponentials(1)
            with act.Fori(0, N_TILES) as n:
                for k in range(CHUNKS_A_TILE):
                    i = n * CHUNKS_A_TILE + k
                    for th in range(NTH):
                        act.wait_ge(third_done, NTH * i + th + 1)
                        if th == 0:
                            act.wait_ge(hid_free[k % 2], n * (CHUNKS_A_TILE // 2) + k // 2 + 1)
                        nc.scalar.activation(hid[k % 2][:, th * TH:(th + 1) * TH], hid_ps[:, th, 0:TH],
                                             ACT.Gelu_apprx_tanh).then_inc(third_out, 1)
                        if th == 0:
                            round_u((k + 1) % 2, i + 2)
                        if th == 0 and k == CHUNKS_A_TILE - 1:
                            exponentials(n + 2)
                        if th == 1:
                            hi_to_block(GROUPS_A_CHUNK * k, n)
                    hi_to_block(GROUPS_A_CHUNK * k + 1, n)
                    if k % 4 == 3:
                        store_block(k // 4, n)
            for group in range(TS // GROUP):
                hi_to_block(group, N_TILES)
            store_block(0, N_TILES)

        @block.tensor
        def _(pe):
            def turn_u(b, n_in):
                pe.wait_ge(u_in[b], n_in)
                for c in range(DC):
                    last = nc.tensor.transpose(turned[:, c, :], raw[b][:, c * P:(c + 1) * P], M.ident[:, :])
                last.then_inc(u_turned, 1)

            def turn_picks(n_probed):
                pe.wait_ge(probed, n_probed)
                for k, src in enumerate((idx[:, 0], idx[:, 1], prob[:, :, :])):
                    last = nc.tensor.transpose(pick_ps[:, k, :], flat(src), M.ident[:, :])
                last.then_inc(picks_turned, 1)

            def weigh(group, n):
                slot = group % SLOTS
                pe.wait_ge(one_made[slot], n * (GROUPS_A_TILE // SLOTS) + group // SLOTS + 1)
                for bank in range(2):
                    pe.wait_ge(w_out[bank], n * GROUPS_A_TILE + group + 1)
                    for t in range(GROUP // 2):
                        at = bank * (GROUP // 2) + t
                        last = nc.tensor.matmul(w_ps[bank][:, t].rearrange("p h i -> p (h i)"), one_j[:, slot, at, :],
                                                one_i[:, slot, at].rearrange("p h i -> p (h i)"), start=True, stop=True)
                    last.then_inc(w_done[bank], 1)

            turn_u(0, 16)
            turn_picks(1)
            with pe.Fori(0, N_TILES) as n:
                for k in range(CHUNKS_A_TILE):
                    i = n * CHUNKS_A_TILE + k
                    pe.wait_ge(u_split, i + 1)
                    for th in range(NTH):
                        pe.wait_ge(third_out, NTH * i + th + 1)
                        last = three_pass(nc, hid_ps[:, th, 0:TH], u_hi[k % 2], u_lo[k % 2], M.x_hi, M.x_lo, th)
                        last.then_inc(third_done, 1)
                        if th == 0:
                            turn_u((k + 1) % 2, 16 * (n * (CHUNKS_A_TILE // 2) + (k + 1) // 2 + 1))
                        elif th == 1:
                            weigh(GROUPS_A_CHUNK * k, n)
                    if k == CHUNKS_A_TILE - 1:
                        turn_picks(n + 2)
                    weigh(GROUPS_A_CHUNK * k + 1, n)
            for group in range(TS // GROUP):
                weigh(group, N_TILES)

        @block.vector
        def _(dve):
            chain = Chain(dve, order)

            def split_u(b, n_round):
                dve.wait_ge(u_round, n_round)
                nc.vector.tensor_tensor(u_lo[b][:, :, :], turned[:, :, :], u_hi[b][:, :, :].bitcast(F32),
                                        ALU.subtract).then_inc(u_split, 1)

            def shift():
                nc.vector.tensor_tensor(prob[:, :, :], best[:, :, :], best[:, :, 0:1].broadcast_to([P, HEADS, TOPK]),
                                        ALU.subtract).then_inc(shifted, 1)

            def softmax(n_tile):
                dve.wait_ge(exped, n_tile)
                chain.step(nc.vector.tensor_reduce(total[:, :], expo[:, :, :], AX_X, ALU.add))
                chain.step(nc.vector.reciprocal(total[:, :], total[:, :]))
                nc.vector.tensor_tensor(prob[:, :, :], expo[:, :, :], total[:, :].unsqueeze(2).broadcast_to([P, HEADS, TOPK]),
                                        ALU.mult).then_inc(probed, 1)

            def picks_by_slot(n_tile):
                dve.wait_ge(picks_turned, n_tile)
                nc.vector.tensor_copy(picks[:, 0:2, :], pick_ps[:, 0:2, :])
                chain.step(nc.vector.tensor_copy(gate_hi[:, :], pick_ps[:, 2, :]))
                nc.vector.tensor_copy(picks[:, 2, :], gate_hi[:, :].bitcast(F32))
                chain.step(nc.vector.tensor_tensor(picks[:, 3, :], pick_ps[:, 2, :], gate_hi[:, :].bitcast(F32), ALU.subtract))

            def one_hots(k, n):
                cur, t0 = curs[k % 2], k * 2 * GROUP
                chain.step(nc.vector.tensor_copy(cur[:, :, :], picks[:, :, t0:t0 + 2 * GROUP]))
                for g in range(GROUPS_A_CHUNK):
                    group = GROUPS_A_CHUNK * k + g
                    slot = group % SLOTS
                    dve.wait_ge(w_done[1], n * GROUPS_A_TILE + group + 1)
                    for t in range(GROUP):
                        at = g * GROUP + t
                        nc.vector.tensor_scalar(one_j[:, slot, t, :], M.iota[:, :], cur[:, 1, at:at + 1], None, ALU.is_equal)
                        for half in range(2):
                            last = nc.vector.tensor_scalar(one_i[:, slot, t, half, :], M.iota[:, :], cur[:, 0, at:at + 1],
                                                           cur[:, 2 + half, at:at + 1], ALU.is_equal, ALU.mult)
                    last.then_inc(one_made[slot], 1)

            def add_lo(group, n):
                for bank in range(2):
                    dve.wait_ge(hi_out[bank], n * GROUPS_A_TILE + group + 1)
                    out, half = block_view(group, bank), w_ps[bank][:, :, 1, :].rearrange("p t (s i) -> p t s i", i=SUPER)
                    nc.vector.tensor_tensor(out, half, out, ALU.add).then_inc(w_out[bank], 1)

            for s in w_done:
                dve.sem_inc(s, SLOTS)
            split_u(0, 1)
            shift()
            softmax(1)
            picks_by_slot(1)
            with dve.Fori(0, N_TILES) as n:
                chain.restart()
                for k in range(CHUNKS_A_TILE):
                    one_hots(k, n)
                    split_u((k + 1) % 2, n * CHUNKS_A_TILE + k + 2)
                    if k == CHUNKS_A_TILE - 2:
                        M.ranking.rank_head(chain, n + 1, HEADS - 1)
                        M.ranking.name_head(chain, HEADS - 1)
                        shift()
                    elif k == CHUNKS_A_TILE - 1:
                        softmax(n + 2)
                    elif k % 2 == 0:
                        M.ranking.rank_head(chain, n + 1, k // 2)
                    else:
                        M.ranking.name_head(chain, k // 2)
                    add_lo(GROUPS_A_CHUNK * k, n)
                    if k == CHUNKS_A_TILE - 1:
                        picks_by_slot(n + 2)
                    add_lo(GROUPS_A_CHUNK * k + 1, n)
            chain.restart()
            for k in range(TS // (2 * GROUP)):
                one_hots(k, N_TILES)
                for g in range(GROUPS_A_CHUNK):
                    add_lo(GROUPS_A_CHUNK * k + g, N_TILES)


def combine(nc, io, M):
    with Phase(nc, "cb") as ph:
        raw = [ph.sb(f"raw{b}", [P, D]) for b in range(2)]
        v_hi = [ph.sb(f"vhi{b}", [P, SUPER, D], F32R) for b in range(2)]
        v_lo = [ph.sb(f"vlo{b}", [P, SUPER, D], F32R) for b in range(2)]
        c_hi = [ph.sb(f"chi{b}", [P, SUPER, T], F32R) for b in range(2)]
        c_lo = [ph.sb(f"clo{b}", [P, SUPER, T], F32R) for b in range(2)]
        wt = [ph.sb(f"wt{b}", [P, TH * SUPER]) for b in range(2)]
        hid = [ph.sb(f"hid{b}", [P, SUPER, TH]) for b in range(2)]
        bank = ph.ps("bank", [P, 8, 512])
        h_in = ph.sem("h_in")
        v_in, v_round, v_split = ph.sems("v_in", 2), ph.sem("v_round"), ph.sem("v_split")
        c_in, c_made, c_round, c_split = ph.sems("c_in", 2), ph.sem("c_made"), ph.sem("c_round"), ph.sem("c_split")
        bank_done, added = ph.sem("bank_done"), ph.sem("added")
        block = ph.block()
        v_rows = io["v_tab"][0].rearrange("(n p) d -> n p d", p=P)
        SUMS = DC * NTH
        supers = NKEYS // SUPER

        @block.sync
        def _(sp):
            start_free(sp, (v_split, v_split, c_split, c_split))
            with sp.Fori(0, supers // 2) as m:
                for b in range(2):
                    def load_third(th):
                        x = NTH * b + th
                        sp.wait_ge(c_split, 2 * NTH * m + x + 1)
                        sp.dma_start(wt[x % 2][:, :], M.weights[bass.ds(2 * m + b, 1), :, th * TH * SUPER:(th + 1) * TH * SUPER]
                                     .rearrange("a j t -> j (a t)")).then_inc(c_in[x % 2], 16)
                        sp.dma_start(hid[x % 2][:, :, :], M.hidden[bass.ds(2 * SUPER * m + SUPER * b, SUPER), :, th * TH:(th + 1) * TH]
                                     .rearrange("i j t -> j i t")).then_inc(c_in[x % 2], 16)

                    def load_v(i):
                        sp.wait_ge(v_split, 2 * SUPER * m + SUPER * b + i + 1)
                        sp.dma_start(raw[i % 2][:, :], v_rows[bass.ds(2 * SUPER * m + SUPER * b + i, 1), :, :]
                                     .rearrange("a p d -> p (a d)")).then_inc(v_in[i % 2], 16)

                    load_third(0)
                    load_v(0)
                    load_v(1)
                    load_third(1)
                    load_v(2)
                    load_third(2)
                    load_v(3)

        @block.gpsimd
        def _(pool):
            with pool.Fori(0, supers // 2) as m:
                for b in range(2):
                    pool.wait_ge(bank_done, 2 * SUMS * m + SUMS * b + 1)
                    for i in range(SUPER):
                        pool.wait_ge(v_in[i % 2], 16 * (SUPER * m + SUPER // 2 * b + i // 2 + 1))
                        pool.sem_inc(M.pool_passed, 1)
                        nc.gpsimd.tensor_copy(v_hi[b][:, i, :], raw[i % 2][:, :]).then_inc(v_round, 1)
                        pool.wait_ge(v_round, 2 * SUPER * m + SUPER * b + i + 1)
                        nc.gpsimd.tensor_tensor(v_lo[b][:, i, :], raw[i % 2][:, :], v_hi[b][:, i, :].bitcast(F32),
                                                ALU.subtract).then_inc(v_split, 1)

        @block.scalar
        def _(act):
            act.wait_ge(c_in[1], 32)
            act.dma_start(M.hT[:, :, :], M.h_spill.rearrange("c p t -> p c t")).then_inc(h_in, 16)
            with act.Fori(0, supers // 2) as m:
                for b in range(2):
                    act.wait_ge(bank_done, 2 * SUMS * m + SUMS * b + 1)
                    for th in range(NTH):
                        x = NTH * b + th
                        act.wait_ge(c_made, 2 * NTH * m + x + 1)
                        nc.scalar.copy(c_hi[b][:, :, th * TH:(th + 1) * TH], hid[x % 2][:, :, :]).then_inc(c_round, 1)

        @block.tensor
        def _(pe):
            pe.sem_inc(bank_done, SUMS + 1)
            pe.sem_inc(added, 8)
            with pe.Fori(0, supers // 2) as m:
                for b in range(2):
                    pe.wait_ge(v_split, 2 * SUPER * m + SUPER * (b + 1) + 2)
                    pe.wait_ge(c_split, 2 * NTH * m + NTH * (b + 1) + 2)
                    for r in range(SUMS):
                        mm, th = divmod(r, NTH)
                        pe.wait_ge(added, 2 * SUMS * m + SUMS * b + r + 1)
                        ws, cols = slice(mm * P, (mm + 1) * P), slice(th * TH, (th + 1) * TH)
                        out = bank[:, r % 8, 0:TH]
                        for i in range(SUPER):
                            nc.tensor.matmul(out, v_hi[b][:, i, ws], c_hi[b][:, i, cols], start=(i == 0), stop=False)
                            nc.tensor.matmul(out, v_hi[b][:, i, ws], c_lo[b][:, i, cols], start=False, stop=False)
                            last = nc.tensor.matmul(out, v_lo[b][:, i, ws], c_hi[b][:, i, cols], start=False, stop=(i == SUPER - 1))
                        last.then_inc(bank_done, 1)

        @block.vector
        def _(dve):
            def make(m, x):
                dve.wait_ge(c_in[x % 2], 32 * (NTH * m + x // 2 + 1))
                nc.vector.tensor_tensor(hid[x % 2][:, :, :], hid[x % 2][:, :, :],
                                        wt[x % 2][:, :].rearrange("p (t i) -> p i t", i=SUPER), ALU.mult).then_inc(c_made, 1)

            def split(m, x):
                b, th = divmod(x, NTH)
                dve.wait_ge(c_round, 2 * NTH * m + x + 1)
                nc.vector.tensor_tensor(c_lo[b][:, :, th * TH:(th + 1) * TH], hid[x % 2][:, :, :],
                                        c_hi[b][:, :, th * TH:(th + 1) * TH].bitcast(F32), ALU.subtract).then_inc(c_split, 1)

            def add(m, b, r):
                mm, th = divmod(r, NTH)
                dve.wait_ge(bank_done, 2 * SUMS * m + SUMS * b + r + 1 + SUMS + 1)
                h = M.hT[:, mm, th * TH:(th + 1) * TH]
                nc.vector.tensor_tensor(h, h, bank[:, r % 8, 0:TH], ALU.add).then_inc(added, 1)

            def step(m, b, ahead):
                for r in range(SUMS):
                    th, odd = divmod(r, 6)
                    if ahead is not None and th < NTH and odd == 0:
                        make(ahead, NTH * (1 - b) + th)
                    if ahead is not None and th < NTH and odd == 4:
                        split(ahead, NTH * (1 - b) + th)
                    add(m, b, r)

            for x in range(NTH):
                make(0, x)
                split(0, x)
            dve.wait_ge(h_in, 16)
            with dve.Fori(0, supers // 2 - 1) as m:
                step(m, 0, m)
                step(m, 1, m + 1)
            step(supers // 2 - 1, 0, supers // 2 - 1)
            step(supers // 2 - 1, 1, None)


def layer_input_gate(nc, io, M):
    with Phase(nc, "pg") as ph:
        ws = WeightStream(nc, ph, io["w_ple_gate"][0], DC)
        KP = D_PLE // P
        p_rows = ph.sb("p_rows", [P, NT, D_PLE])
        pT = ph.sb("pT", [P, KP, T])
        wp = [ph.sb(f"wp{b}", [P, KP, P]) for b in range(2)]
        sig = [ph.sb(f"sig{b}", [P, T]) for b in range(2)]
        gate, proj = ph.ps("gate", [P, NTH, 512]), ph.ps("proj", [P, NTH, 512])
        turn = ph.ps("turn", [P, 2, 512])
        p_in, p_turned, p_out = ph.sem("p_in"), ph.sem("p_turned"), ph.sem("p_out")
        wp_in, proj_done, sigmoid, gated, added = ph.sems("wp_in", 2), ph.sem("proj_done"), ph.sem("sigmoid"), ph.sem("gated"), ph.sem("added")
        block = ph.block()
        wp_cols = io["w_ple_proj"][0].rearrange("(c p) e -> p c e", p=P)

        @block.sync
        def _(sp):
            sp.dma_start(p_rows[:, 0:N_TILES, :], io["p_prompt"][0, 0].rearrange("(n p) e -> p n e", p=P)).then_inc(p_in, 16)
            sp.dma_start(p_rows[0:TS, N_TILES, :], io["p_sample"][0].rearrange("b s e -> (b s) e")).then_inc(p_in, 16)
            ws.start(sp)
            start_free(sp, (proj_done, proj_done))
            with sp.Fori(0, ws.pairs) as n:
                for b in range(2):
                    ws.load(sp, n, b)
                    sp.wait_ge(proj_done, 2 * n + b + 1)
                    sp.dma_start(wp[b][:, :, :], wp_cols[:, :, bass.ds(2 * P * n + P * b, P)]).then_inc(wp_in[b], 16)

        @block.gpsimd
        def _(pool):
            with pool.Fori(0, ws.pairs) as n:
                for b in range(2):
                    ws.halve(pool, n, b)

        @block.tensor
        def _(pe):
            pe.wait_ge(p_in, 32)
            for r in range(NT):
                if r >= 2:
                    pe.wait_ge(p_out, r - 1)
                rows = P if r < N_TILES else TS
                for k in range(KP):
                    last = nc.tensor.transpose(turn[:, r % 2, k * P:k * P + rows], p_rows[0:rows, r, k * P:(k + 1) * P],
                                               M.ident[0:rows, 0:rows])
                last.then_inc(p_turned, 1)
            pe.wait_ge(p_out, NT)
            start_free(pe, (sigmoid, gated))
            with pe.Fori(0, ws.pairs) as n:
                for b in range(2):
                    pe.wait_ge(sigmoid, 2 * n + b + 1)
                    ws.product(pe, n, b, gate, M.x_hi, M.x_lo)
                    pe.wait_ge(wp_in[b], 16 * n + 16)
                    pe.wait_ge(gated, 2 * n + b + 1)
                    for th in range(NTH):
                        for k in range(KP):
                            last = nc.tensor.matmul(proj[:, th, 0:TH], wp[b][:, k, :], pT[:, k, th * TH:(th + 1) * TH],
                                                    start=(k == 0), stop=(k == KP - 1))
                    last.then_inc(proj_done, 1)

        @block.scalar
        def _(act):
            for r in range(NT):
                act.wait_ge(p_turned, r + 1)
                rows = P if r < N_TILES else TS
                nc.scalar.copy(pT[:, :, r * P:r * P + rows],
                               turn[:, r % 2, 0:2 * P].rearrange("p (k t) -> p k t", k=KP)[:, :, 0:rows]).then_inc(p_out, 1)
            start_free(act, (added, added))
            with act.Fori(0, ws.pairs) as n:
                for b in range(2):
                    act.wait_ge(ws.used[b], n + 2)
                    act.wait_ge(added, 2 * n + b + 1)
                    nc.scalar.activation(thirds(sig[b][:, :]), gate[:, :, 0:TH], ACT.Sigmoid).then_inc(sigmoid, 1)

        @block.vector
        def _(dve):
            with dve.Fori(0, ws.pairs) as n:
                for b in range(2):
                    dve.wait_ge(sigmoid, 2 * n + b + 2)
                    dve.wait_ge(proj_done, 2 * n + b + 3)
                    nc.vector.tensor_tensor(thirds(sig[b][:, :]), thirds(sig[b][:, :]), proj[:, :, 0:TH], ALU.mult).then_inc(gated, 1)
                    dve.wait_ge(gated, 2 * n + b + 2)
                    row = M.hT[:, bass.ds(2 * n + b, 1), :].rearrange("p o t -> p (o t)")
                    nc.vector.tensor_tensor(row, row, sig[b][:, :], ALU.add).then_inc(added, 1)


def store_rows(nc, io, M, yT):
    with Phase(nc, "st") as ph:
        y = [ph.sb(f"y{b}", [P, D]) for b in range(2)]
        turn = [ph.ps(f"turn{b}", [P, DC, P]) for b in range(2)]
        turned, copied, stored = ph.sem("turned"), ph.sem("copied"), ph.sems("stored", 2)
        block = ph.block()

        @block.tensor
        def _(pe):
            for t in range(NT):
                rows = P if t < N_TILES else TS
                if t >= 2:
                    pe.wait_ge(copied, t - 1)
                for c in range(DC):
                    last = nc.tensor.transpose(turn[t % 2][0:rows, c, :], yT[:, c, t * P:t * P + rows], M.ident[:, :])
                last.then_inc(turned, 1)

        @block.scalar
        def _(act):
            for t in range(NT):
                rows = P if t < N_TILES else TS
                act.wait_ge(turned, t + 1)
                if t >= 2:
                    act.wait_ge(stored[t % 2], 16 * (t // 2))
                nc.scalar.copy(y[t % 2][0:rows, :], flat(turn[t % 2][0:rows, :, :])).then_inc(copied, 1)

        @block.sync
        def _(sp):
            for t in range(NT):
                sp.wait_ge(copied, t + 1)
                if t < N_TILES:
                    sp.dma_start(io["y_prompt"][0, t * P:(t + 1) * P, :], y[t % 2][:, :]).then_inc(stored[t % 2], 16)
                else:
                    sp.dma_start(io["y_sample"].rearrange("b s d -> (b s) d"), y[t % 2][0:TS, :]).then_inc(stored[t % 2], 16)
            sp.wait_ge(stored[0], 16 * ((NT + 1) // 2))
            sp.wait_ge(stored[1], 16 * (NT // 2))


def spill_h(nc, M):
    with Phase(nc, "sh") as ph:
        spilled = ph.sem("spilled")
        block = ph.block()

        @block.sync
        def _(sp):
            sp.dma_start(M.h_spill.rearrange("c p t -> p c t"), M.hT[:, :, :]).then_inc(spilled, 16)
            sp.wait_ge(spilled, 16)


def clear_ended(nc, spared):
    with nc.Block() as block:

        @block.sync
        def _(sp):
            for s in ENDED:
                if s not in spared:
                    sp.sem_clear(s)
    ENDED.clear()


class Memory:
    pass


def decoder_step(nc, io):
    ENDED.clear()
    with Phase(nc, "m") as ph:
        M = Memory()
        M.hidden = nc.dram_tensor("hidden", (NKEYS, P, T), F32).ap()
        M.weights = nc.dram_tensor("weights", (NKEYS // SUPER, P, T * SUPER), F32).ap()
        M.h_spill = nc.dram_tensor("h_spill", (DC, P, T), F32).ap()
        M.ident, M.iota = ph.sb("ident", [P, P]), ph.sb("iota", [P, P])
        M.mean_d, M.mean_c = ph.sb("mean_d", [P, P]), ph.sb("mean_c", [P, P])
        M.vec = ph.sb("vec", [P, NVEC])
        M.pool_passed, M.dve_passed = ph.sem("pool_passed"), ph.sem("dve_passed")
        with Phase(nc, "m1") as p1:
            M.x_hi, M.x_lo = p1.sb("x_hi", [P, DC, T], F32R), p1.sb("x_lo", [P, DC, T], F32R)
            with Phase(nc, "m2") as p2:
                M.hT = p2.sb("hT", [P, DC, T])
                M.mix = p2.sb("mix", [P, DC, T])
                M.taps = p2.sb("taps", [P, MC, TAPS + 1])
                M.pool_pre = p2.sb("pool_pre", [P, MC, DEC_B * POOL_PRE])
                M.conv_pre = p2.sb("conv_pre", [P, MC, DEC_B * CONV_PRE])
                M.plast = p2.sb("plast", [P, MC, POOL_PRE * (1 + DEC_B)])
                M.ulast = p2.sb("ulast", [P, MC, CONV_PRE * (1 + DEC_B)])
                load_inputs(nc, io, M)
                normalise(nc, M, "n1", VEC["g_mix"], hi=M.x_hi, lo=M.x_lo)
                mixer(nc, io, M)
                mixer_tail(nc, io, M)
                out_projection(nc, io, M)
                normalise(nc, M, "n2", VEC["g_ffn"], hi=M.x_hi, lo=M.x_lo)
                spill_h(nc, M)
            with Phase(nc, "m3") as p3:
                M.sv, M.si = p3.sb("sv", [P, NT, 2 * HEADS, TOPK]), p3.sb("si", [P, NT, 2 * HEADS, TOPK])
                M.ranking = Ranking(nc, p3, M)
                key_scores(nc, io, M)
                hidden_and_weights(nc, io, M)
        with Phase(nc, "m4") as p4:
            M.hT = p4.sb("hT", [P, DC, T])
            clear_ended(nc, (M.pool_passed, M.dve_passed))
            combine(nc, io, M)
            with Phase(nc, "m5") as p5:
                M.x_hi, M.x_lo = p5.sb("x_hi", [P, DC, T], F32R), p5.sb("x_lo", [P, DC, T], F32R)
                normalise(nc, M, "n3", VEC["g_ple"], hi=M.x_hi, lo=M.x_lo)
                layer_input_gate(nc, io, M)
            yT = p4.sb("yT", [P, DC, T])
            normalise(nc, M, "n4", VEC["g_final"], plain=yT)
            store_rows(nc, io, M, yT)


_OUTS = [("y_prompt", (1, SEQ, D)), ("y_sample", (DEC_B, DEC_S, D)),
         ("pool_state_prompt", (1, 1, POOL_PRE, D_HALF_MIX)), ("conv_state_prompt", (1, 1, CONV_PRE, D_HALF_MIX)),
         ("pool_state_sample", (1, DEC_B, POOL_PRE, D_HALF_MIX)), ("conv_state_sample", (1, DEC_B, CONV_PRE, D_HALF_MIX))]
_INS = ["x_prompt", "x_sample", "state_pool", "state_conv", "p_prompt", "p_sample", "g_mix", "w_in", "w_pool", "pool_scale",
        "w_dw", "b_dw", "ln_g", "ln_b", "w_out", "g_ffn", "w_q", "sub_keys", "u_tab", "v_tab", "g_ple", "w_ple_gate",
        "w_ple_proj", "g_final"]


def kernel(**inputs):
    import numpy as _np
    import concourse.bacc as _bacc
    from concourse import mybir as _mybir
    from concourse.bass_utils import run_bass_kernel_spmd as _run

    nc = _bacc.Bacc("TRN2", target_bir_lowering=False, num_devices=1)
    arrays, io = {}, {}
    for name in _INS:
        a = _np.ascontiguousarray(inputs[name])
        arrays[f"in_{name}_dram"] = a
        io[name] = nc.dram_tensor(f"in_{name}_dram", a.shape, _mybir.dt.from_np(a.dtype), kind="ExternalInput").ap()
    for name, shape in _OUTS:
        io[name] = nc.dram_tensor(f"out_{name}_dram", shape, _mybir.dt.float32, kind="ExternalOutput").ap()
    decoder_step(nc, io)
    r = _run(nc, [arrays], core_ids=[0])
    return tuple(r.results[0][f"out_{name}_dram"] for name, _ in _OUTS)
```

```python
from contextlib import ExitStack

import concourse.bass as bass
from concourse import mybir

ALU = mybir.AluOpType
ACT = mybir.ActivationFunctionType
AX_X = mybir.AxisListType.X
F32 = mybir.dt.float32
F32R = mybir.dt.float32r
U32 = mybir.dt.uint32

P = 128
D = 1024
DC = D // P
SEQ = 1024
DEC_B, DEC_S = 8, 4
TS = DEC_B * DEC_S
T = SEQ + TS
NTH = 3
TH = T // NTH
NT = SEQ // P + 1
LAST = SEQ - 2 * TH
D_HALF_MIX = 512
MC = D_HALF_MIX // P
WINDOWS = (2, 4, 8, 16)
POOL_PRE = max(WINDOWS) - 1
TAPS = 31
CONV_PRE = TAPS - 1
D_PLE = 256
HEADS = 8
TOPK = 16
NKEYS = 128
EPS = 1e-6
NEG = -3.0e38
GROUP = 4
SUPER = 4
BLOCK_T = 32

VEC = {"g_mix": 0, "g_ffn": 8, "g_ple": 16, "g_final": 24, "pool_scale": 32, "b_dw": 36, "ln_g": 40, "ln_b": 44}
NVEC = 48


class Chain:

    def __init__(self, eng, sem):
        self.eng, self.sem, self.n = eng, sem, 0

    def restart(self):
        self.eng.sem_clear(self.sem)
        self.n = 0

    def step(self, ins):
        self.n += 1
        ins.then_inc(self.sem, 1)
        self.eng.wait_ge(self.sem, self.n)


ENDED = []


class Phase:

    def __init__(self, nc, name):
        self.nc, self.name, self.ctx = nc, name, ExitStack()

    def __enter__(self):
        self.ctx.__enter__()
        return self

    def __exit__(self, *a):
        return self.ctx.__exit__(*a)

    def sb(self, name, shape, dt=F32):
        return self.ctx.enter_context(self.nc.sbuf_tensor(f"{self.name}_{name}", shape, dt))

    def ps(self, name, shape):
        return self.ctx.enter_context(self.nc.psum_tensor(f"{self.name}_{name}", shape, F32))

    def sem(self, name):
        s = self.ctx.enter_context(self.nc.semaphore(f"{self.name}_{name}"))
        ENDED.append(s)
        return s

    def sems(self, name, n):
        return [self.sem(f"{name}{i}") for i in range(n)]

    def block(self):
        return self.ctx.enter_context(self.nc.Block())


def start_free(eng, sems):
    for s in sems:
        eng.sem_inc(s, 1)


def thirds(ap):
    return ap.rearrange("p (a b) -> p a b", a=NTH)


def flat(ap):
    return ap.rearrange("p a b -> p (a b)")


def flat4(ap):
    return ap.rearrange("p a b c -> p (a b) c")


def load_inputs(nc, io, M):
    with Phase(nc, "ld") as ph:
        xin = [ph.sb(f"xin{b}", [P, D]) for b in range(2)]
        xlast = ph.sb("xlast", [TS, D])
        vecs = ph.sb("vecs", [NVEC, P])
        taps = ph.sb("taps", [TAPS, D_HALF_MIX])
        spool = ph.sb("spool", [DEC_B * POOL_PRE, D_HALF_MIX])
        sconv = ph.sb("sconv", [DEC_B * CONV_PRE // 2, 2, D_HALF_MIX])
        turned = [ph.ps(f"turned{b}", [P, DC, P]) for b in range(2)]
        small = [ph.ps(f"small{b}", [P, 512]) for b in range(2)]
        x_in = ph.sems("x_in", 2)
        x_turned = ph.sems("x_turned", 2)
        x_out = ph.sems("x_out", 2)
        xlast_in, small_in = ph.sem("xlast_in"), ph.sem("small_in")
        const0, consts = ph.sem("const0"), ph.sem("consts")
        small_turned, small_out = ph.sem("small_turned"), ph.sem("small_out")
        sq = [ph.sb(f"sq{b}", [P, DC, P]) for b in range(2)]
        sq_last = ph.sb("sq_last", [P, DC, TS])
        sq_used, order = ph.sems("sq_used", 2), ph.sem("order")
        block = ph.block()
        xp = io["x_prompt"][0].rearrange("(n p) d -> n p d", p=P)

        @block.sync
        def _(sp):
            with sp.Fori(0, SEQ // P // 2) as n:
                for b in range(2):
                    sp.wait_ge(x_out[b], n + 1)
                    sp.dma_start(xin[b][:, :], xp[bass.ds(2 * n + b, 1), :, :].rearrange("a p d -> p (a d)")).then_inc(x_in[b], 16)
            sp.dma_start(xlast[:, :], io["x_sample"].rearrange("b s d -> (b s) d")).then_inc(xlast_in, 16)

        @block.gpsimd
        def _(pool):
            nc.gpsimd.memset(M.ident[:, :], 0.0).then_inc(const0, 1)
            pool.wait_ge(const0, 1)
            nc.gpsimd.affine_select(out=M.ident[:, :], in_=M.ident[:, :], compare_op=ALU.not_equal, fill=1.0,
                                    base=0, pattern=[[-1, P]], channel_multiplier=1).then_inc(consts, 1)
            nc.gpsimd.memset(M.eps[:, :], EPS)
            nc.gpsimd.memset(M.mean_d[:, :], 1.0 / D).then_inc(consts, 1)
            nc.gpsimd.memset(M.mean_c[:, :], 1.0 / D_HALF_MIX).then_inc(consts, 1)
            nc.gpsimd.iota(M.iota[:, :], [[1, P]], base=0, channel_multiplier=0,
                           allow_small_or_imprecise_dtypes=True).then_inc(consts, 1)

        @block.scalar
        def _(act):
            for name, row in VEC.items():
                src = io[name] if name == "g_final" else io[name][0]
                k = src.shape[0] // P
                act.dma_start(vecs[row:row + k, :], src.rearrange("(c p) -> c p", p=P)).then_inc(small_in, 16)
            act.dma_start(taps[:, :], io["w_dw"][0]).then_inc(small_in, 16)
            act.dma_start(spool[:, :], io["state_pool"][0].rearrange("b s c -> (b s) c")).then_inc(small_in, 16)
            for h in range(2):
                act.dma_start(sconv[:, h, :], io["state_conv"][0].rearrange("b s c -> (b s) c")[
                    h * 120:(h + 1) * 120, :]).then_inc(small_in, 16)
            with act.Fori(0, SEQ // P // 2) as n:
                for b in range(2):
                    act.wait_ge(x_turned[b], n + 1)
                    act.nop()
                    nc.scalar.copy(M.hT[:, :, bass.ds(n * 2 * P + b * P, P)], turned[b][:, :, :])
                    act.wait_ge(sq_used[b], n + 1)
                    nc.scalar.activation(sq[b][:, :, :], turned[b][:, :, :], ACT.Square).then_inc(x_out[b], 1)

        @block.tensor
        def _(pe):
            pe.wait_ge(consts, 4)
            start_free(pe, x_out)
            with pe.Fori(0, SEQ // P // 2) as n:
                for b in range(2):
                    pe.wait_ge(x_in[b], 16 * n + 16)
                    pe.wait_ge(x_out[b], n + 1)
                    for c in range(DC):
                        last = nc.tensor.transpose(turned[b][:, c, :], xin[b][:, c * P:(c + 1) * P], M.ident[:, :])
                    last.then_inc(x_turned[b], 1)
            pe.wait_ge(xlast_in, 16)
            pe.wait_ge(x_out[0], 1 + SEQ // P // 2)
            for c in range(DC):
                last = nc.tensor.transpose(turned[0][:, c, 0:TS], xlast[:, c * P:(c + 1) * P], M.ident[0:TS, 0:TS])
            last.then_inc(small_turned, 1)
            pe.wait_ge(small_in, 16 * (len(VEC) + 4))
            nc.tensor.transpose(small[0][:, 0:NVEC], vecs[:, :], M.ident[0:NVEC, 0:NVEC])
            for c in range(MC):
                last = nc.tensor.transpose(small[0][:, 64 + 32 * c:64 + 32 * c + TAPS], taps[:, c * P:(c + 1) * P],
                                           M.ident[0:TAPS, 0:TAPS])
            last.then_inc(small_turned, 1)
            n_pool = DEC_B * POOL_PRE
            for c in range(MC):
                last = nc.tensor.transpose(small[1][:, n_pool * c:n_pool * (c + 1)], spool[:, c * P:(c + 1) * P],
                                           M.ident[0:n_pool, 0:n_pool])
            last.then_inc(small_turned, 1)
            for h in range(2):
                pe.wait_ge(small_out, 2 + h)
                for c in range(MC):
                    last = nc.tensor.transpose(small[h][:, 120 * c:120 * (c + 1)], sconv[:, h, c * P:(c + 1) * P],
                                               M.ident[0:120, 0:120])
                last.then_inc(small_turned, 1)

        @block.vector
        def _(dve):
            chain = Chain(dve, order)
            start_free(dve, sq_used)
            with dve.Fori(0, SEQ // P // 2) as n:
                for b in range(2):
                    dve.wait_ge(x_out[b], n + 2)
                    dve.sem_inc(M.dve_passed, 1)
                    nc.vector.tensor_reduce(M.total[:, bass.ds(n * 2 * P + b * P, P)],
                                            sq[b][:, :, :].rearrange("p c t -> p t c"), AX_X, ALU.add).then_inc(sq_used[b], 1)
            dve.wait_ge(small_turned, 1)
            chain.step(nc.vector.tensor_copy(M.hT[:, :, SEQ:T], turned[0][:, :, 0:TS]))
            chain.step(nc.vector.tensor_tensor(sq_last[:, :, :], M.hT[:, :, SEQ:T], M.hT[:, :, SEQ:T], ALU.mult))
            nc.vector.tensor_reduce(M.total[:, SEQ:T], sq_last[:, :, :].rearrange("p c t -> p t c"), AX_X, ALU.add)
            dve.wait_ge(small_turned, 2)
            nc.vector.tensor_copy(M.vec[:, :], small[0][:, 0:NVEC]).then_inc(small_out, 1)
            nc.vector.tensor_copy(M.taps[:, :, 0:TAPS], small[0][:, 64:192].rearrange("p (c k) -> p c k", c=MC)[
                :, :, 0:TAPS]).then_inc(small_out, 1)
            dve.wait_ge(small_turned, 3)
            nc.vector.tensor_copy(flat(M.pool_pre[:, :, :]), small[1][:, 0:480]).then_inc(small_out, 1)
            for h in range(2):
                dve.wait_ge(small_turned, 4 + h)
                nc.vector.tensor_copy(M.conv_pre[:, :, 120 * h:120 * (h + 1)],
                                      small[h][:, 0:480].rearrange("p (c k) -> p c k", c=MC))
            dve.wait_ge(small_out, 3)
            nc.vector.tensor_copy(M.taps[:, :, TAPS:TAPS + 1], M.vec[:, VEC["b_dw"]:VEC["b_dw"] + MC].rearrange(
                "p (c k) -> p c k", k=1))


class SquareSum:

    def __init__(self, nc, ph, M, buffers):
        self.nc, self.M, self.buffers = nc, M, buffers
        self.squared, self.summed = ph.sem("sq_squared"), ph.sem("sq_summed")

    def start(self, pool):
        self.nc.gpsimd.memset(self.M.total[:, :], 0.0).then_inc(self.summed, 1)
        pool.wait_ge(self.summed, 1)
        pool.sem_inc(self.summed, 1)

    def square(self, act, i, b):
        act.wait_ge(self.summed, i + 1)
        act.nop()
        self.nc.scalar.activation(self.buffers[b][:, :].rearrange("p (o t) -> p o t", o=1), self.M.hT[:, bass.ds(i, 1), :],
                                  ACT.Square).then_inc(self.squared, 1)

    def add(self, dve, i, b):
        dve.wait_ge(self.squared, i + 1)
        dve.wait_ge(self.summed, i + 2)
        self.nc.vector.tensor_tensor(self.M.total[:, :], self.M.total[:, :], self.buffers[b][:, :],
                                     ALU.add).then_inc(self.summed, 1)


class WeightStream:

    def __init__(self, nc, ph, w, chunks):
        self.nc, self.pairs = nc, chunks // 2
        self.cols = w.rearrange("(c p) e -> p c e", p=P)
        self.raw = [ph.sb(f"raw{b}", [P, DC, P]) for b in range(2)]
        self.hi = [ph.sb(f"whi{b}", [P, DC, P], F32R) for b in range(2)]
        self.lo = [ph.sb(f"wlo{b}", [P, DC, P], F32R) for b in range(2)]
        self.loaded = ph.sems("w_loaded", 2)
        self.rounded = ph.sems("w_rounded", 2)
        self.split = ph.sems("w_split", 2)
        self.used = ph.sems("w_used", 2)
        self.passed = ph.sem("w_passed")

    def start(self, sp):
        start_free(sp, self.split + self.used)

    def load(self, sp, n, b):
        sp.wait_ge(self.split[b], n + 1)
        sp.dma_start(self.raw[b][:, :, :], self.cols[:, :, bass.ds(n * 2 * P + b * P, P)]).then_inc(self.loaded[b], 16)

    def load_first(self, sp):
        self.start(sp)
        for b in range(2):
            self.load(sp, 0, b)

    def load_rest(self, sp):
        with sp.Fori(1, self.pairs) as n:
            for b in range(2):
                self.load(sp, n, b)

    def halve_rest(self, pool):
        self.halve(pool, 0, 1)
        with pool.Fori(1, self.pairs) as n:
            for b in range(2):
                self.halve(pool, n, b)

    def halve(self, pool, n, b):
        pool.wait_ge(self.loaded[b], 16 * n + 16)
        pool.wait_ge(self.used[b], n + 1)
        pool.sem_inc(self.passed, 1)
        self.nc.gpsimd.tensor_copy(self.hi[b][:, :, :], self.raw[b][:, :, :]).then_inc(self.rounded[b], 1)
        pool.wait_ge(self.rounded[b], n + 1)
        self.nc.gpsimd.tensor_tensor(flat(self.lo[b][:, :, :]), flat(self.raw[b][:, :, :]),
                                     flat(self.hi[b][:, :, :]).bitcast(F32), ALU.subtract).then_inc(self.split[b], 1)

    def product(self, pe, n, b, out, x_hi, x_lo, third_done=None):
        pe.wait_ge(self.split[b], n + 2)
        for th in range(NTH):
            last = three_pass(self.nc, out[:, th, 0:TH], self.hi[b], self.lo[b], x_hi, x_lo, th)
            if third_done is not None and th < NTH - 1:
                last.then_inc(third_done, 1)
        last.then_inc(self.used[b], 1)


def normalise(nc, M, name, gain, hi, lo, spill=None, ahead=None):
    with Phase(nc, name) as ph:
        NB = 4
        on_pool = (0, 3, 5) if ahead is None else (0, 3)
        x = [ph.sb(f"x{b}", [P, T]) for b in range(NB)]
        std, rstd = ph.sb("std", [P, T]), ph.sb("rstd", [P, T])
        mean = ph.ps("mean", [P, NTH, 512])
        summed, rooted, inverted = ph.sem("summed"), ph.sem("rooted"), ph.sem("inverted")
        scaled, rounded, split, pool_split = ph.sem("scaled"), ph.sem("rounded"), ph.sem("split"), ph.sem("pool_split")
        spilled = ph.sem("spilled")
        block = ph.block()

        @block.sync
        def _(sp):
            if ahead is not None:
                ahead.load_first(sp)
            if spill is not None:
                sp.dma_start(spill.rearrange("c p t -> p c t"), M.hT[:, :, :]).then_inc(spilled, 16)
                sp.wait_ge(spilled, 16)

        @block.scalar
        def _(act):
            for th in range(NTH):
                act.wait_ge(summed, th + 1)
                nc.scalar.activation(std[:, th * TH:(th + 1) * TH], mean[:, th, 0:TH], ACT.Sqrt,
                                     bias=M.eps[:, 0:1]).then_inc(rooted, 1)
            for c in range(DC):
                act.wait_ge(scaled, c + 1)
                nc.scalar.copy(hi[:, c, :], x[c % NB][:, :]).then_inc(rounded, 1)

        @block.tensor
        def _(pe):
            for th in range(NTH):
                nc.tensor.matmul(mean[:, th, 0:TH], M.mean_d[:, :], M.total[:, th * TH:(th + 1) * TH],
                                 start=True, stop=True).then_inc(summed, 1)

        @block.gpsimd
        def _(pool):
            for c in on_pool:
                pool.wait_ge(rounded, c + 1)
                nc.gpsimd.tensor_tensor(lo[:, c, :], x[c % NB][:, :], hi[:, c, :].bitcast(F32),
                                        ALU.subtract).then_inc(pool_split, 1)
            if ahead is not None:
                ahead.halve(pool, 0, 0)

        @block.vector
        def _(dve):
            for th in range(NTH):
                dve.wait_ge(rooted, th + 1)
                nc.vector.reciprocal(rstd[:, th * TH:(th + 1) * TH], std[:, th * TH:(th + 1) * TH]).then_inc(inverted, 1)
            dve.wait_ge(inverted, NTH)

            def free(c):
                if c in on_pool:
                    dve.wait_ge(pool_split, sum(k <= c for k in on_pool))
                else:
                    dve.wait_ge(split, sum(k not in on_pool for k in range(c + 1)))

            def subtract(c):
                if c not in on_pool:
                    dve.wait_ge(rounded, c + 1)
                    nc.vector.tensor_tensor(lo[:, c, :], x[c % NB][:, :], hi[:, c, :].bitcast(F32),
                                            ALU.subtract).then_inc(split, 1)

            for c in range(DC):
                if c >= 2:
                    subtract(c - 2)
                if c >= NB:
                    free(c - NB)
                nc.vector.scalar_tensor_tensor(out=x[c % NB][:, :], in0=M.hT[:, c, :], scalar=M.vec[:, gain + c:gain + c + 1],
                                               in1=rstd[:, :], op0=ALU.mult, op1=ALU.mult).then_inc(scaled, 1)
            subtract(DC - 2)
            subtract(DC - 1)


def three_pass(nc, out, w_hi, w_lo, x_hi, x_lo, th, first=True, final=True):
    cols = slice(th * TH, (th + 1) * TH)
    for c in range(DC):
        nc.tensor.matmul(out, w_hi[:, c, :], x_hi[:, c, cols], start=(first and c == 0), stop=False)
        nc.tensor.matmul(out, w_hi[:, c, :], x_lo[:, c, cols], start=False, stop=False)
        last = nc.tensor.matmul(out, w_lo[:, c, :], x_hi[:, c, cols], start=False, stop=(final and c == DC - 1))
    return last


def mixer(nc, io, M):
    with Phase(nc, "mx") as ph:
        raw = [ph.sb(f"raw{k}", [P, DC, P]) for k in range(2)]
        w_hi = [ph.sb(f"whi{k}", [P, DC, P], F32R) for k in range(2)]
        w_lo = [ph.sb(f"wlo{k}", [P, DC, P], F32R) for k in range(2)]
        pfull = ph.sb("pfull", [P, MC, POOL_PRE + SEQ])
        pfull_s = ph.sb("pfulls", [P, MC, DEC_B, POOL_PRE + DEC_S])
        ufull = ph.sb("ufull", [P, CONV_PRE + SEQ])
        ufull_s = ph.sb("ufulls", [P, DEC_B, CONV_PRE + DEC_S])
        tap = ph.sb("tap", [P, TAPS + 1])
        sig = ph.sb("sig", [P, T])
        conv = ph.sb("conv", [P, T])
        count = ph.sb("count", [P, 16])
        part_s = ph.sb("parts", [P, 2, DEC_B, POOL_PRE + DEC_S])
        val, gate = ph.ps("val", [P, NTH, 512]), ph.ps("gate", [P, NTH, 512])
        pool_ps = ph.ps("pool", [P, 2, 512])
        w_in = ph.sems("w_in", 2)
        w_round = ph.sems("w_round", 2)
        w_split = ph.sems("w_split", 2)
        w_used = ph.sems("w_used", 2)
        sigmoid, gated, conved, moved = ph.sem("sigmoid"), ph.sem("gated"), ph.sem("conved"), ph.sem("moved")
        saved = ph.sem("saved")
        third_done, third_out = ph.sem("third_done"), ph.sem("third_out")
        order, order_s = ph.sem("order"), ph.sem("order_s")
        state_turned, state_copied, state_out = ph.sem("state_turned"), ph.sem("state_copied"), ph.sem("state_out")
        pool_order = ph.sem("pool_order")
        pooled = ph.sem("pooled")
        block = ph.block()
        w_cols = io["w_in"][0].rearrange("(c p) e -> p c e", p=P)

        @block.sync
        def _(sp):
            start_free(sp, w_split)
            with sp.Fori(0, MC) as c:
                for k in range(2):
                    sp.wait_ge(w_split[k], c + 1)
                    sp.dma_start(raw[k][:, :, :], w_cols[:, :, bass.ds(D_HALF_MIX * (1 + k) + c * P, P)]).then_inc(w_in[k], 16)
            for g in range(MC):
                k = g % 2
                sp.wait_ge(w_split[k], MC + g // 2 + 1)
                sp.dma_start(raw[k][:, :, :], w_cols[:, :, g * P:(g + 1) * P]).then_inc(w_in[k], 16)

        @block.gpsimd
        def _(pool):
            nc.gpsimd.memset(ufull[:, 0:CONV_PRE], 0.0).then_inc(pool_order, 1)
            nc.gpsimd.memset(pfull[:, :, 0:POOL_PRE], 0.0).then_inc(pool_order, 1)

            def split_weights(k, loaded, rounded):
                pool.wait_ge(w_in[k], loaded)
                pool.sem_inc(M.pool_passed, 1)
                nc.gpsimd.tensor_copy(w_hi[k][:, :, :], raw[k][:, :, :]).then_inc(w_round[k], 1)
                pool.wait_ge(w_round[k], rounded)
                nc.gpsimd.tensor_tensor(flat(w_lo[k][:, :, :]), flat(raw[k][:, :, :]),
                                        flat(w_hi[k][:, :, :]).bitcast(F32), ALU.subtract).then_inc(w_split[k], 1)

            start_free(pool, w_used)
            with pool.Fori(0, MC) as c:
                for k in range(2):
                    pool.wait_ge(w_used[k], c + 1)
                    split_weights(k, 16 * c + 16, c + 1)
                pool.wait_ge(gated, c + 2)
                pool.sem_inc(M.pool_passed, 1)
                nc.gpsimd.tensor_copy(M.ulast[:, bass.ds(c, 1), 0:CONV_PRE],
                                      ufull[:, SEQ:SEQ + CONV_PRE].rearrange("p (a b) -> p a b", a=1)).then_inc(saved, 1)
                nc.gpsimd.tensor_copy(
                    M.ulast[:, bass.ds(c, 1), CONV_PRE:CONV_PRE * 9].rearrange("p a (b s) -> p (a b) s", b=DEC_B),
                    ufull_s[:, :, DEC_S:DEC_S + CONV_PRE]).then_inc(saved, 1)
            for g in range(MC):
                k, uses = g % 2, MC + g // 2
                if g < 2:
                    pool.wait_ge(w_used[k], MC + 1)
                else:
                    pool.wait_ge(third_done, NTH * (g - 1))
                split_weights(k, 16 * (uses + 1), uses + 1)

        @block.scalar
        def _(act):
            with act.Fori(0, MC) as c:
                act.wait_ge(w_used[1], c + 2)
                act.wait_ge(gated, c + 1)
                nc.scalar.activation(thirds(sig[:, :]), gate[:, :, 0:TH], ACT.Sigmoid).then_inc(sigmoid, 1)
                act.wait_ge(conved, 2 * c + 2)
                act.nop()
                nc.scalar.copy(M.mix[:, bass.ds(c + MC, 1), :], conv[:, :].rearrange("p (a b) -> p a b", a=1)).then_inc(moved, 1)
            for g in range(MC):
                for th in range(NTH):
                    act.wait_ge(third_done, NTH * g + th + 1)
                    ps = pool_ps[:, th % 2, 0:TH]
                    if th < 2:
                        nc.scalar.copy(pfull[:, g, POOL_PRE + th * TH:POOL_PRE + (th + 1) * TH], ps).then_inc(third_out, 1)
                    else:
                        nc.scalar.copy(pfull[:, g, POOL_PRE + 2 * TH:POOL_PRE + SEQ], ps[:, 0:LAST]).then_inc(pooled, 1)
                        nc.scalar.copy(pfull_s[:, g, :, POOL_PRE:POOL_PRE + DEC_S],
                                       ps[:, LAST:TH].rearrange("p (b s) -> p b s", b=DEC_B)).then_inc(third_out, 1)

        @block.tensor
        def _(pe):
            with pe.Fori(0, MC) as c:
                for k, out in ((0, val), (1, gate)):
                    pe.wait_ge(w_split[k], c + 2)
                    pe.wait_ge(gated, c + 1)
                    for th in range(NTH):
                        last = three_pass(nc, out[:, th, 0:TH], w_hi[k], w_lo[k], M.x_hi, M.x_lo, th)
                    last.then_inc(w_used[k], 1)
            for g in range(MC):
                k = g % 2
                pe.wait_ge(w_split[k], MC + g // 2 + 2)
                for th in range(NTH):
                    need = NTH * g + (th - 1 if th == 2 else 0)
                    if need:
                        pe.wait_ge(third_out, need)
                    last = three_pass(nc, pool_ps[:, th % 2, 0:TH], w_hi[k], w_lo[k], M.x_hi, M.x_lo, th)
                    last.then_inc(third_done, 1)

        @block.vector
        def _(dve):
            dve.wait_ge(pool_order, 2)
            chain, chain_s = Chain(dve, order), Chain(dve, order_s)
            start_free(dve, (gated, saved, moved))
            with dve.Fori(0, MC) as c:
                chain.restart()
                chain_s.restart()
                dve.wait_ge(sigmoid, c + 1)
                dve.wait_ge(saved, 2 * c + 1)
                nc.vector.tensor_tensor(ufull[:, CONV_PRE:CONV_PRE + 2 * TH].rearrange("p (a b) -> p a b", a=2),
                                        val[:, 0:2, 0:TH], sig[:, 0:2 * TH].rearrange("p (a b) -> p a b", a=2), ALU.mult)
                nc.vector.tensor_tensor(ufull[:, CONV_PRE + 2 * TH:CONV_PRE + SEQ], val[:, 2, 0:LAST],
                                        sig[:, 2 * TH:SEQ], ALU.mult)
                nc.vector.tensor_copy(tap[:, :].rearrange("p (a b) -> p a b", a=1), M.taps[:, bass.ds(c, 1), :])
                nc.vector.tensor_copy(ufull_s[:, :, 0:CONV_PRE], M.conv_pre[:, bass.ds(c, 1), :].rearrange(
                    "p a (b s) -> p (a b) s", b=DEC_B))
                nc.vector.tensor_tensor(ufull_s[:, :, CONV_PRE:CONV_PRE + DEC_S],
                                        val[:, 2, LAST:TH].rearrange("p (b s) -> p b s", b=DEC_B),
                                        sig[:, SEQ:T].rearrange("p (b s) -> p b s", b=DEC_B), ALU.mult).then_inc(gated, 1)
                dve.wait_ge(gated, c + 2)
                dve.wait_ge(moved, c + 1)
                out_s = conv[:, SEQ:T].rearrange("p (b s) -> p b s", b=DEC_B)
                for k in range(TAPS):
                    src, src_s = ufull[:, k:k + SEQ], ufull_s[:, :, k:k + DEC_S]
                    if k == 0:
                        a = nc.vector.tensor_scalar(conv[:, 0:SEQ], src, tap[:, 0:1], tap[:, TAPS:TAPS + 1], ALU.mult, ALU.add)
                        b = nc.vector.tensor_scalar(out_s, src_s, tap[:, 0:1], tap[:, TAPS:TAPS + 1], ALU.mult, ALU.add)
                        a.then_inc(order, 1)
                        b.then_inc(order_s, 1)
                    else:
                        done, done_s = (order, order_s) if k < TAPS - 1 else (conved, conved)
                        dve.wait_ge(order, k)
                        nc.vector.scalar_tensor_tensor(out=conv[:, 0:SEQ], in0=src, scalar=tap[:, k:k + 1],
                                                       in1=conv[:, 0:SEQ], op0=ALU.mult, op1=ALU.add).then_inc(done, 1)
                        dve.wait_ge(order_s, k)
                        nc.vector.scalar_tensor_tensor(out=out_s, in0=src_s, scalar=tap[:, k:k + 1],
                                                       in1=out_s, op0=ALU.mult, op1=ALU.add).then_inc(done_s, 1)
            chain.restart()
            dve.wait_ge(moved, MC + 1)
            for g, w in enumerate(WINDOWS):
                dve.wait_ge(third_out, NTH * (g + 1))
                dve.wait_ge(pooled, g + 1)
                chain.step(nc.vector.tensor_copy(pfull_s[:, g, :, 0:POOL_PRE], M.pool_pre[:, g, :].rearrange(
                    "p (b s) -> p b s", b=DEC_B)))
                cur, cur_s = pfull[:, g, :], pfull_s[:, g]
                n, n_s, m = POOL_PRE + SEQ, POOL_PRE + DEC_S, 0
                while (1 << m) < w:
                    d = 1 << m
                    nxt = (conv, sig)[m % 2][:, 0:n - d]
                    nxt_s = part_s[:, m % 2, :, 0:n_s - d]
                    nc.vector.tensor_tensor(nxt, cur[:, d:n], cur[:, 0:n - d], ALU.add)
                    chain.step(nc.vector.tensor_tensor(nxt_s, cur_s[:, :, d:n_s], cur_s[:, :, 0:n_s - d], ALU.add))
                    cur, cur_s, n, n_s, m = nxt, nxt_s, n - d, n_s - d, m + 1
                chain.step(nc.vector.tensor_scalar(count[:, 0:16], M.iota[:, 0:16], 1.0, float(w), ALU.add, ALU.min))
                chain.step(nc.vector.reciprocal(count[:, 0:16], count[:, 0:16]))
                at = n - SEQ
                chain.step(nc.vector.tensor_tensor(count[:, 0:16], cur[:, at:at + 16], count[:, 0:16], ALU.mult))
                nc.vector.tensor_tensor(M.mix[:, g, 0:16], count[:, 0:16], pfull[:, g, POOL_PRE:POOL_PRE + 16], ALU.subtract)
                nc.vector.scalar_tensor_tensor(out=M.mix[:, g, 16:SEQ], in0=cur[:, at + 16:at + SEQ], scalar=1.0 / w,
                                               in1=pfull[:, g, POOL_PRE + 16:POOL_PRE + SEQ], op0=ALU.mult, op1=ALU.subtract)
                at = n_s - DEC_S
                chain.step(nc.vector.scalar_tensor_tensor(
                    out=M.mix[:, g, SEQ:T].rearrange("p (b s) -> p b s", b=DEC_B), in0=cur_s[:, :, at:n_s], scalar=1.0 / w,
                    in1=pfull_s[:, g, :, POOL_PRE:POOL_PRE + DEC_S], op0=ALU.mult, op1=ALU.subtract))
                nc.vector.tensor_copy(M.plast[:, g, 0:POOL_PRE], pfull[:, g, SEQ:SEQ + POOL_PRE])
                chain.step(nc.vector.tensor_copy(M.plast[:, g, POOL_PRE:POOL_PRE * 9].rearrange("p (b s) -> p b s", b=DEC_B),
                                                 pfull_s[:, g, :, DEC_S:DEC_S + POOL_PRE]))


def mixer_tail(nc, io, M, ahead):
    with Phase(nc, "mt") as ph:
        wp = ph.sb("wp", [P, MC, P])
        sq = [ph.sb(f"sq{b}", [P, T]) for b in range(2)]
        std, rstd = ph.sb("std", [P, T]), ph.sb("rstd", [P, T])
        prow = ph.sb("prow", [P, 2, D_HALF_MIX])
        crow = ph.sb("crow", [P, 3, D_HALF_MIX])
        mean = ph.ps("mean", [P, NTH, 512])
        ya = ph.ps("ya", [P, NTH, 512])
        rows = ph.ps("rows", [P, 2, 512])
        wp_in, rows_turned, rows_copied, rows_out = ph.sem("wp_in"), ph.sem("rows_turned"), ph.sem("rows_copied"), ph.sem("rows_out")
        ya_done, ya_out = ph.sem("ya_done"), ph.sem("ya_out")
        meaned, centred, squared, summed = ph.sem("meaned"), ph.sem("centred"), ph.sem("squared"), ph.sem("summed")
        inverted, rooted, normed, rounded = ph.sem("inverted"), ph.sem("rooted"), ph.sem("normed"), ph.sem("rounded")
        swished = ph.sem("swished")
        block = ph.block()
        n_pool, n_conv = DEC_B * POOL_PRE, DEC_B * CONV_PRE // 2
        jobs = [(M.plast, 0, POOL_PRE, prow, 0), (M.plast, POOL_PRE, n_pool, prow, 1),
                (M.ulast, 0, CONV_PRE, crow, 0), (M.ulast, CONV_PRE, n_conv, crow, 1),
                (M.ulast, CONV_PRE + n_conv, n_conv, crow, 2)]
        cs = io["conv_state_sample"][0].rearrange("b s c -> (b s) c")
        dests = [io["pool_state_prompt"][0, 0], io["pool_state_sample"][0].rearrange("b s c -> (b s) c"),
                 io["conv_state_prompt"][0, 0], cs[0:n_conv, :], cs[n_conv:2 * n_conv, :]]

        @block.sync
        def _(sp):
            sp.dma_start(wp[:, :, :], io["w_pool"][0].rearrange("g c d -> c g d")).then_inc(wp_in, 16)
            ahead.load_first(sp)
            for j, (_, _, n, row, r) in enumerate(jobs):
                sp.wait_ge(rows_copied, j + 1)
                sp.dma_start(dests[j], row[0:n, r, :]).then_inc(rows_out, 16)
            sp.wait_ge(rows_out, 16 * len(jobs))

        @block.gpsimd
        def _(pool):
            ahead.halve(pool, 0, 0)
            for g in range(MC):
                pool.wait_ge(rounded, g + 1)
                nc.gpsimd.tensor_tensor(M.x_lo[:, g, :], M.mix[:, g, :], M.x_hi[:, g, :].bitcast(F32), ALU.subtract)

        @block.tensor
        def _(pe):
            def pooled_map(g):
                for th in range(NTH):
                    last = nc.tensor.matmul(ya[:, th, 0:TH], wp[:, g, :], M.mix[:, g, th * TH:(th + 1) * TH],
                                            start=True, stop=True)
                last.then_inc(ya_done, 1)

            for c in range(MC):
                for th in range(NTH):
                    last = nc.tensor.matmul(mean[:, th, 0:TH], M.mean_c[:, :], M.mix[:, MC + c, th * TH:(th + 1) * TH],
                                            start=(c == 0), stop=(c == MC - 1))
            last.then_inc(meaned, 1)
            pe.wait_ge(wp_in, 16)
            pooled_map(0)
            pe.wait_ge(centred, MC)
            for c in range(MC):
                pe.wait_ge(squared, c + 1)
                for th in range(NTH):
                    last = nc.tensor.matmul(mean[:, th, 0:TH], M.mean_c[:, :], sq[c % 2][:, th * TH:(th + 1) * TH],
                                            start=(c == 0), stop=(c == MC - 1))
                last.then_inc(summed, 1)
            for g in range(1, MC):
                pe.wait_ge(ya_out, g)
                pooled_map(g)
            for j, (src, at, n, _, _) in enumerate(jobs):
                if j >= 2:
                    pe.wait_ge(rows_copied, j - 1)
                for c in range(MC):
                    last = nc.tensor.transpose(rows[0:n, j % 2, c * P:(c + 1) * P], src[:, c, at:at + n], M.ident[:, :])
                last.then_inc(rows_turned, 1)

        @block.scalar
        def _(act):
            def scale_group(g):
                act.wait_ge(ya_done, g + 1)
                nc.scalar.activation(thirds(M.mix[:, g, :]), ya[:, :, 0:TH], ACT.Copy,
                                     scale=M.vec[:, VEC["pool_scale"] + g:VEC["pool_scale"] + g + 1]).then_inc(ya_out, 1)

            scale_group(0)
            for c in range(MC):
                act.wait_ge(centred, c + 1)
                if c >= 2:
                    act.wait_ge(summed, c - 1)
                nc.scalar.activation(sq[c % 2][:, :], M.mix[:, MC + c, :], ACT.Square).then_inc(squared, 1)
            act.wait_ge(summed, MC)
            nc.scalar.activation(thirds(std[:, :]), mean[:, :, 0:TH], ACT.Sqrt, bias=M.eps[:, 0:1]).then_inc(rooted, 1)
            for g in range(MC):
                if g:
                    scale_group(g)
                act.wait_ge(ya_out, g + 1)
                nc.scalar.copy(M.x_hi[:, g, :], M.mix[:, g, :]).then_inc(rounded, 1)
            for c in range(MC):
                act.wait_ge(normed, c + 1)
                nc.scalar.activation(M.mix[:, MC + c, :], M.mix[:, MC + c, :], ACT.Silu,
                                     scale=M.vec[:, VEC["ln_g"] + c:VEC["ln_g"] + c + 1],
                                     bias=M.vec[:, VEC["ln_b"] + c:VEC["ln_b"] + c + 1]).then_inc(swished, 1)
                act.wait_ge(swished, c + 1)
                nc.scalar.copy(M.x_hi[:, MC + c, :], M.mix[:, MC + c, :]).then_inc(rounded, 1)

        @block.vector
        def _(dve):
            dve.wait_ge(meaned, 1)
            for c in range(MC):
                nc.vector.tensor_tensor(thirds(M.mix[:, MC + c, :]), thirds(M.mix[:, MC + c, :]), mean[:, :, 0:TH],
                                        ALU.subtract).then_inc(centred, 1)
            dve.wait_ge(rooted, 1)
            nc.vector.reciprocal(rstd[:, :], std[:, :]).then_inc(inverted, 1)
            dve.wait_ge(inverted, 1)
            for c in range(MC):
                nc.vector.tensor_tensor(M.mix[:, MC + c, :], M.mix[:, MC + c, :], rstd[:, :], ALU.mult).then_inc(normed, 1)
            for j, (_, _, n, row, r) in enumerate(jobs):
                dve.wait_ge(rows_turned, j + 1)
                nc.vector.tensor_copy(row[0:n, r, :], rows[0:n, j % 2, :]).then_inc(rows_copied, 1)
            for c in range(MC, DC):
                dve.wait_ge(rounded, c + 1)
                nc.vector.tensor_tensor(M.x_lo[:, c, :], M.mix[:, c, :], M.x_hi[:, c, :].bitcast(F32), ALU.subtract)


def out_projection(nc, M, ws):
    with Phase(nc, "op") as ph:
        out = [ph.ps(f"out{b}", [P, NTH, 512]) for b in range(2)]
        added = ph.sems("added", 2)
        squares = SquareSum(nc, ph, M, [ph.sb(f"sq{b}", [P, T]) for b in range(2)])
        block = ph.block()

        @block.sync
        def _(sp):
            ws.load_rest(sp)

        @block.gpsimd
        def _(pool):
            squares.start(pool)
            ws.halve_rest(pool)

        @block.scalar
        def _(act):
            with act.Fori(0, ws.pairs) as n:
                for b in range(2):
                    act.wait_ge(added[b], n + 2)
                    squares.square(act, 2 * n + b, b)

        @block.tensor
        def _(pe):
            start_free(pe, added)
            with pe.Fori(0, ws.pairs) as n:
                for b in range(2):
                    pe.wait_ge(added[b], n + 1)
                    ws.product(pe, n, b, out[b], M.x_hi, M.x_lo)

        @block.vector
        def _(dve):
            with dve.Fori(0, ws.pairs) as n:
                for b in range(2):
                    dve.wait_ge(ws.used[b], n + 2)
                    row = M.hT[:, bass.ds(2 * n + b, 1), :].rearrange("p o (a b) -> p (o a) b", a=NTH)
                    nc.vector.tensor_tensor(row, row, out[b][:, :, 0:TH], ALU.add).then_inc(added[b], 1)
                    squares.add(dve, 2 * n + b, b)


class Ranking:

    def __init__(self, nc, ph, M):
        self.nc, self.M = nc, M
        self.key_s, self.key_at = ph.sb("key_s", [P, 2, TOPK]), ph.sb("key_at", [P, 2, TOPK])
        self.cand, self.rest = ph.sb("cand", [P, TOPK, TOPK]), ph.sb("rest", [P, TOPK * TOPK])
        self.top, self.top_at = ph.sb("top", [P, TOPK]), ph.sb("top_at", [P, TOPK], U32)
        self.rank = ph.sb("rank", [P, 2, TOPK], U32)
        self.same = ph.sb("same", [P, 2, TOPK, TOPK])
        self.best, self.idx = ph.sb("best", [P, HEADS, TOPK]), ph.sb("idx", [P, 2, HEADS, TOPK])

    def rank_head(self, chain, tile, head):
        self.nc.vector.tensor_copy(self.key_s[:, :, :], flat4(self.M.sv[:, bass.ds(tile, 1), bass.ds(2 * head, 2), :]))
        chain.step(self.nc.vector.tensor_copy(self.key_at[:, :, :], flat4(self.M.si[:, bass.ds(tile, 1), bass.ds(2 * head, 2), :])))
        chain.step(self.nc.vector.tensor_tensor(
            self.cand[:, :, :], self.key_s[:, 0, :].unsqueeze(2).broadcast_to([P, TOPK, TOPK]),
            self.key_s[:, 1, :].unsqueeze(1).broadcast_to([P, TOPK, TOPK]), ALU.add))
        chain.step(self.nc.vector.max(self.top[:, 0:8], flat(self.cand[:, :, :])))
        self.nc.vector.max_index(self.top_at[:, 0:8], self.top[:, 0:8], flat(self.cand[:, :, :]))
        chain.step(self.nc.vector.match_replace(self.rest[:, :], self.top[:, 0:8], flat(self.cand[:, :, :]), NEG))
        chain.step(self.nc.vector.max(self.top[:, 8:16], self.rest[:, :]))
        chain.step(self.nc.vector.max_index(self.top_at[:, 8:16], self.top[:, 8:16], self.rest[:, :]))

    def name_head(self, chain, head):
        self.nc.vector.tensor_copy(self.best[:, bass.ds(head, 1), :], self.top[:, :].unsqueeze(1))
        self.nc.vector.tensor_scalar(self.rank[:, 0, :], self.top_at[:, :], 4, None, ALU.logical_shift_right)
        chain.step(self.nc.vector.tensor_scalar(self.rank[:, 1, :], self.top_at[:, :], TOPK - 1, None, ALU.bitwise_and))
        for w in range(2):
            last = self.nc.vector.tensor_tensor(self.same[:, w], self.M.iota[:, 0:TOPK].unsqueeze(1).broadcast_to([P, TOPK, TOPK]),
                                           self.rank[:, w, :].unsqueeze(2).broadcast_to([P, TOPK, TOPK]), ALU.is_equal)
        chain.step(last)
        for w in range(2):
            last = self.nc.vector.tensor_tensor(self.same[:, w], self.same[:, w],
                                           self.key_at[:, w, :].unsqueeze(1).broadcast_to([P, TOPK, TOPK]), ALU.mult)
        chain.step(last)
        for w in range(2):
            last = self.nc.vector.tensor_reduce(self.idx[:, w, bass.ds(head, 1), :].rearrange("p a k -> p (a k)"),
                                           self.same[:, w], AX_X, ALU.add)
        chain.step(last)


def key_scores(nc, io, M):
    with Phase(nc, "ks") as ph:
        ws = WeightStream(nc, ph, io["w_q"][0], 2 * HEADS)
        keys = ph.sb("keys", [P, 2 * HEADS, P])
        keysT = ph.sb("keysT", [P, 2 * HEADS, P])
        qT = [ph.sb(f"qT{b}", [P, T]) for b in range(2)]
        score = [ph.sb(f"score{b}", [P, NT, NKEYS]) for b in range(2)]
        rest = ph.sb("rest", [P, NT, NKEYS])
        top = ph.sb("top", [P, NT, TOPK])
        top_at = ph.sb("top_at", [P, NT, TOPK], U32)
        q_ps = ph.ps("q", [P, NTH, 512])
        s_ps = ph.ps("s", [P, 3, 512])
        k_ps = ph.ps("k", [P, 2, 512])
        keys_in, keys_turned, keys_out = ph.sem("keys_in"), ph.sem("keys_turned"), ph.sem("keys_out")
        q_out, third_done = ph.sem("q_out"), ph.sem("third_done")
        scored = ph.sem("scored")
        score_out = ph.sem("score_out")
        picked = ph.sem("picked")
        order = ph.sem("order")
        cleared = ph.sem("cleared")
        block = ph.block()

        @block.sync
        def _(sp):
            sp.dma_start(keys[:, :, :], io["sub_keys"][0].rearrange("h s k c -> k (h s) c")).then_inc(keys_in, 16)
            ws.start(sp)
            with sp.Fori(0, ws.pairs) as n:
                for b in range(2):
                    ws.load(sp, n, b)

        @block.gpsimd
        def _(pool):
            for b in range(2):
                nc.gpsimd.memset(score[b][:, NT - 1, :], 0.0).then_inc(cleared, 1)
            with pool.Fori(0, ws.pairs) as n:
                for b in range(2):
                    ws.halve(pool, n, b)

        @block.tensor
        def _(pe):
            pe.wait_ge(keys_in, 16)
            for r in range(4):
                if r >= 2:
                    pe.wait_ge(keys_out, r - 1)
                for k in range(4):
                    last = nc.tensor.transpose(k_ps[:, r % 2, k * P:(k + 1) * P], keys[:, 4 * r + k, :], M.ident[:, :])
                last.then_inc(keys_turned, 1)
            pe.wait_ge(keys_out, 4)

            def scores(b, n_q, n_free, index):
                pe.wait_ge(q_out, n_q)
                pe.wait_ge(score_out, n_free)
                for t in range(NT):
                    rows = P if t < NT - 1 else TS
                    last = nc.tensor.matmul(s_ps[0:rows, t // 4, (t % 4) * P:(t % 4 + 1) * P], qT[b][:, t * P:t * P + rows],
                                            keysT[:, bass.ds(index, 1), :].rearrange("p a k -> p (a k)"),
                                            start=True, stop=True)
                last.then_inc(scored, 1)

            start_free(pe, (score_out,))
            with pe.Fori(0, ws.pairs) as n:
                for b in range(2):
                    ws.product(pe, n, b, q_ps, M.x_hi, M.x_lo, third_done)
                    scores(b, 6 * n + 3 * b + 3, 2 * n + b + 1, 2 * n + b)

        @block.scalar
        def _(act):
            for r in range(4):
                act.wait_ge(keys_turned, r + 1)
                nc.scalar.copy(keysT[:, 4 * r:4 * r + 4, :], k_ps[:, r % 2, :].rearrange("p (a b) -> p a b", a=4)).then_inc(keys_out, 1)
            act.wait_ge(cleared, 2)
            start_free(act, (scored, scored, picked, picked))
            with act.Fori(0, ws.pairs) as n:
                for b in range(2):
                    act.wait_ge(scored, 2 * n + b + 1)
                    for th in range(NTH):
                        if th < NTH - 1:
                            act.wait_ge(third_done, 4 * n + 2 * b + th + 1)
                        else:
                            act.wait_ge(ws.used[b], n + 2)
                        nc.scalar.copy(qT[b][:, th * TH:(th + 1) * TH], q_ps[:, th, 0:TH]).then_inc(q_out, 1)
                    act.wait_ge(scored, 2 * n + b + 3)
                    act.wait_ge(picked, 2 * n + b + 1)
                    nc.scalar.copy(score[b][:, 0:8, :].rearrange("p (a c) k -> p a c k", a=2),
                                   s_ps[:, 0:2, :].rearrange("p a (c k) -> p a c k", c=4))
                    nc.scalar.copy(score[b][0:TS, 8, :], s_ps[0:TS, 2, 0:P]).then_inc(score_out, 1)

        @block.vector
        def _(dve):
            chain = Chain(dve, order)
            with dve.Fori(0, ws.pairs) as n:
                chain.restart()
                for b in range(2):
                    dve.wait_ge(picked, 2 * n + b + 2)
                    dve.wait_ge(score_out, 2 * n + b + 2)
                    dve.sem_inc(M.dve_passed, 1)
                    s = score[b]
                    for t in range(NT):
                        last = nc.vector.max(top[:, t, 0:8], s[:, t, :])
                    chain.step(last)
                    for t in range(NT):
                        nc.vector.max_index(top_at[:, t, 0:8], top[:, t, 0:8], s[:, t, :])
                        last = nc.vector.match_replace(rest[:, t, :], top[:, t, 0:8], s[:, t, :], NEG)
                    chain.step(last)
                    for t in range(NT):
                        last = nc.vector.max(top[:, t, 8:16], rest[:, t, :])
                    chain.step(last)
                    for t in range(NT):
                        last = nc.vector.max_index(top_at[:, t, 8:16], top[:, t, 8:16], rest[:, t, :])
                    chain.step(last)
                    nc.vector.tensor_copy(M.sv[:, :, bass.ds(2 * n + b, 1), :].rearrange("p t a k -> p t (a k)"), top[:, :, :])
                    nc.vector.tensor_copy(M.si[:, :, bass.ds(2 * n + b, 1), :].rearrange("p t a k -> p t (a k)"),
                                          top_at[:, :, :]).then_inc(picked, 1)
                dve.wait_ge(picked, 2 * n + 4)
                dve.sem_inc(M.dve_passed, 1)
                M.ranking.rank_head(chain, 0, n)
                M.ranking.name_head(chain, n)


CHUNKS_A_TILE = NKEYS // (SEQ // P)
GROUPS_A_CHUNK = 2
GROUPS_A_TILE = GROUPS_A_CHUNK * CHUNKS_A_TILE
BLOCKS_A_TILE = P // BLOCK_T
SLOTS = 4
N_TILES = SEQ // P
BLOCKS = T // BLOCK_T


def hidden_and_weights(nc, io, M):
    with Phase(nc, "hw") as ph:
        raw = [ph.sb(f"raw{b}", [P, D]) for b in range(2)]
        u_hi = [ph.sb(f"uhi{b}", [P, DC, P], F32R) for b in range(2)]
        u_lo = [ph.sb(f"ulo{b}", [P, DC, P], F32R) for b in range(2)]
        hid = [ph.sb(f"hid{b}", [P, T]) for b in range(2)]
        weight = [ph.sb(f"wt{b}", [P, NKEYS // SUPER, BLOCK_T * SUPER]) for b in range(2)]
        one_j = ph.sb("one_j", [P, SLOTS, GROUP, NKEYS], F32R)
        one_i = ph.sb("one_i", [P, SLOTS, GROUP, 2, NKEYS], F32R)
        picks = ph.sb("picks", [P, 4, P])
        gate_hi = ph.sb("gate_hi", [P, P], F32R)
        curs = [ph.sb(f"cur{b}", [P, 4, 2 * GROUP]) for b in range(2)]
        best, idx = M.ranking.best, M.ranking.idx
        prob, expo = ph.sb("prob", [P, HEADS, TOPK]), ph.sb("expo", [P, HEADS, TOPK])
        total = ph.sb("total", [P, HEADS])

        hid_ps = ph.ps("hid", [P, NTH, 512])
        turned = ph.ps("turned", [P, DC, P])
        w_ps = [ph.ps(f"w{b}", [P, GROUP // 2, 2, NKEYS]) for b in range(2)]
        pick_ps = ph.ps("pick", [P, 4, P])

        u_in, u_turned = ph.sems("u_in", 2), ph.sem("u_turned")
        u_round, u_split = ph.sem("u_round"), ph.sem("u_split")
        third_done, third_out = ph.sem("third_done"), ph.sem("third_out")
        hid_stored, hid_free = ph.sems("hid_stored", 2), ph.sems("hid_free", 2)
        one_made = ph.sems("one_made", SLOTS)
        w_done, hi_out, w_out, w_stored = ph.sems("w_done", 2), ph.sems("hi_out", 2), ph.sems("w_out", 2), ph.sems("w_stored", 2)
        shifted, exped, probed, picks_turned = ph.sem("shifted"), ph.sem("exped"), ph.sem("probed"), ph.sem("picks_turned")
        order = ph.sem("order")
        block = ph.block()
        u_rows = io["u_tab"][0].rearrange("(n p) d -> n p d", p=P)

        def block_view(group, bank):
            t0 = (group % 8 * GROUP + bank * (GROUP // 2)) * SUPER
            return weight[group // 8 % 2][:, :, t0:t0 + GROUP // 2 * SUPER].rearrange("p s (t i) -> p t s i", i=SUPER)

        @block.sync
        def _(sp):
            start_free(sp, (u_turned, u_turned))
            with sp.Fori(0, NKEYS // 2) as n:
                for b in range(2):
                    sp.wait_ge(u_turned, 2 * n + b + 1)
                    sp.dma_start(raw[b][:, :], u_rows[bass.ds(2 * n + b, 1), :, :].rearrange("a p d -> p (a d)")).then_inc(u_in[b], 16)
            sp.wait_ge(u_turned, NKEYS + 1)
            sp.dma_start(raw[0][:, :], u_rows[0]).then_inc(u_in[0], 16)

        @block.gpsimd
        def _(pool):
            with pool.Fori(0, NKEYS // 2) as n:
                for b in range(2):
                    pool.wait_ge(third_out, NTH * (2 * n + b + 2))
                    pool.dma_start(M.hidden[bass.ds(2 * n + b, 1), :, :].rearrange("a p t -> p (a t)"),
                                   hid[b][:, :]).then_inc(hid_stored[b], 16)
                    pool.wait_ge(hid_stored[b], 16 * n + 16)
                    pool.sem_inc(hid_free[b], 1)
            for b in range(2):
                pool.wait_ge(w_stored[b], 16 * ((BLOCKS + 1 - b) // 2 + 1))

        @block.scalar
        def _(act):
            def round_u(b, n_turned):
                act.wait_ge(u_turned, n_turned + 2)
                nc.scalar.copy(u_hi[b][:, :, :], turned[:, :, :]).then_inc(u_round, 1)

            def hi_to_block(group, n):
                blk = group // 8
                if group % 8 == 0:
                    act.wait_ge(w_stored[blk % 2], 16 * (n * (BLOCKS_A_TILE // 2) + blk // 2 + 1))
                for bank in range(2):
                    act.wait_ge(w_done[bank], n * GROUPS_A_TILE + group + SLOTS + 1)
                    half = w_ps[bank][:, :, 0, :].rearrange("p t (s i) -> p t s i", i=SUPER)
                    nc.scalar.copy(block_view(group, bank), half).then_inc(hi_out[bank], 1)

            def store_block(blk, n):
                for bank in range(2):
                    act.wait_ge(w_out[bank], n * GROUPS_A_TILE + 8 * blk + 9)
                act.dma_start(M.weights[:, :, bass.ds((n * BLOCKS_A_TILE + blk) * (BLOCK_T * SUPER), BLOCK_T * SUPER)].rearrange(
                    "s j t -> j s t"), weight[blk % 2][:, :, :]).then_inc(w_stored[blk % 2], 16)

            def exponentials(n_shifted):
                act.wait_ge(shifted, n_shifted)
                nc.scalar.activation(expo[:, :, :], prob[:, :, :], ACT.Exp).then_inc(exped, 1)

            start_free(act, (third_out,) * NTH)
            start_free(act, hid_free + w_out)
            for s in w_stored:
                act.sem_inc(s, 16)
            round_u(0, 1)
            exponentials(1)
            with act.Fori(0, N_TILES) as n:
                for k in range(CHUNKS_A_TILE):
                    i = n * CHUNKS_A_TILE + k
                    for th in range(NTH):
                        act.wait_ge(third_done, NTH * i + th + 1)
                        if th == 0:
                            act.wait_ge(hid_free[k % 2], n * (CHUNKS_A_TILE // 2) + k // 2 + 1)
                        nc.scalar.activation(hid[k % 2][:, th * TH:(th + 1) * TH], hid_ps[:, th, 0:TH],
                                             ACT.Gelu_apprx_tanh).then_inc(third_out, 1)
                        if th == 0:
                            round_u((k + 1) % 2, i + 2)
                        if th == 0 and k == CHUNKS_A_TILE - 1:
                            exponentials(n + 2)
                        if th == 1:
                            hi_to_block(GROUPS_A_CHUNK * k, n)
                    hi_to_block(GROUPS_A_CHUNK * k + 1, n)
                    if k % 4 == 3:
                        store_block(k // 4, n)
            for group in range(TS // GROUP):
                hi_to_block(group, N_TILES)
            store_block(0, N_TILES)

        @block.tensor
        def _(pe):
            def turn_u(b, n_in):
                pe.wait_ge(u_in[b], n_in)
                for c in range(DC):
                    last = nc.tensor.transpose(turned[:, c, :], raw[b][:, c * P:(c + 1) * P], M.ident[:, :])
                last.then_inc(u_turned, 1)

            def turn_picks(n_probed):
                pe.wait_ge(probed, n_probed)
                for k, src in enumerate((idx[:, 0], idx[:, 1], prob[:, :, :])):
                    last = nc.tensor.transpose(pick_ps[:, k, :], flat(src), M.ident[:, :])
                last.then_inc(picks_turned, 1)

            def weigh(group, n):
                slot = group % SLOTS
                pe.wait_ge(one_made[slot], n * (GROUPS_A_TILE // SLOTS) + group // SLOTS + 1)
                for bank in range(2):
                    pe.wait_ge(w_out[bank], n * GROUPS_A_TILE + group + 1)
                    for t in range(GROUP // 2):
                        at = bank * (GROUP // 2) + t
                        last = nc.tensor.matmul(w_ps[bank][:, t].rearrange("p h i -> p (h i)"), one_j[:, slot, at, :],
                                                one_i[:, slot, at].rearrange("p h i -> p (h i)"), start=True, stop=True)
                    last.then_inc(w_done[bank], 1)

            turn_u(0, 16)
            turn_picks(1)
            with pe.Fori(0, N_TILES) as n:
                for k in range(CHUNKS_A_TILE):
                    i = n * CHUNKS_A_TILE + k
                    pe.wait_ge(u_split, i + 1)
                    for th in range(NTH):
                        pe.wait_ge(third_out, NTH * i + th + 1)
                        last = three_pass(nc, hid_ps[:, th, 0:TH], u_hi[k % 2], u_lo[k % 2], M.x_hi, M.x_lo, th)
                        last.then_inc(third_done, 1)
                        if th == 0:
                            turn_u((k + 1) % 2, 16 * (n * (CHUNKS_A_TILE // 2) + (k + 1) // 2 + 1))
                        elif th == 1:
                            weigh(GROUPS_A_CHUNK * k, n)
                    if k == CHUNKS_A_TILE - 1:
                        turn_picks(n + 2)
                    weigh(GROUPS_A_CHUNK * k + 1, n)
            for group in range(TS // GROUP):
                weigh(group, N_TILES)

        @block.vector
        def _(dve):
            chain = Chain(dve, order)

            def split_u(b, n_round):
                dve.wait_ge(u_round, n_round)
                nc.vector.tensor_tensor(u_lo[b][:, :, :], turned[:, :, :], u_hi[b][:, :, :].bitcast(F32),
                                        ALU.subtract).then_inc(u_split, 1)

            def shift():
                nc.vector.tensor_tensor(prob[:, :, :], best[:, :, :], best[:, :, 0:1].broadcast_to([P, HEADS, TOPK]),
                                        ALU.subtract).then_inc(shifted, 1)

            def softmax(n_tile):
                dve.wait_ge(exped, n_tile)
                chain.step(nc.vector.tensor_reduce(total[:, :], expo[:, :, :], AX_X, ALU.add))
                chain.step(nc.vector.reciprocal(total[:, :], total[:, :]))
                nc.vector.tensor_tensor(prob[:, :, :], expo[:, :, :], total[:, :].unsqueeze(2).broadcast_to([P, HEADS, TOPK]),
                                        ALU.mult).then_inc(probed, 1)

            def picks_by_slot(n_tile):
                dve.wait_ge(picks_turned, n_tile)
                nc.vector.tensor_copy(picks[:, 0:2, :], pick_ps[:, 0:2, :])
                chain.step(nc.vector.tensor_copy(gate_hi[:, :], pick_ps[:, 2, :]))
                nc.vector.tensor_copy(picks[:, 2, :], gate_hi[:, :].bitcast(F32))
                chain.step(nc.vector.tensor_tensor(picks[:, 3, :], pick_ps[:, 2, :], gate_hi[:, :].bitcast(F32), ALU.subtract))

            def one_hots(k, n):
                cur, t0 = curs[k % 2], k * 2 * GROUP
                chain.step(nc.vector.tensor_copy(cur[:, :, :], picks[:, :, t0:t0 + 2 * GROUP]))
                for g in range(GROUPS_A_CHUNK):
                    group = GROUPS_A_CHUNK * k + g
                    slot = group % SLOTS
                    dve.wait_ge(w_done[1], n * GROUPS_A_TILE + group + 1)
                    for t in range(GROUP):
                        at = g * GROUP + t
                        nc.vector.tensor_scalar(one_j[:, slot, t, :], M.iota[:, :], cur[:, 1, at:at + 1], None, ALU.is_equal)
                        for half in range(2):
                            last = nc.vector.tensor_scalar(one_i[:, slot, t, half, :], M.iota[:, :], cur[:, 0, at:at + 1],
                                                           cur[:, 2 + half, at:at + 1], ALU.is_equal, ALU.mult)
                    last.then_inc(one_made[slot], 1)

            def add_lo(group, n):
                for bank in range(2):
                    dve.wait_ge(hi_out[bank], n * GROUPS_A_TILE + group + 1)
                    out, half = block_view(group, bank), w_ps[bank][:, :, 1, :].rearrange("p t (s i) -> p t s i", i=SUPER)
                    nc.vector.tensor_tensor(out, half, out, ALU.add).then_inc(w_out[bank], 1)

            for s in w_done:
                dve.sem_inc(s, SLOTS)
            split_u(0, 1)
            shift()
            softmax(1)
            picks_by_slot(1)
            with dve.Fori(0, N_TILES) as n:
                chain.restart()
                for k in range(CHUNKS_A_TILE):
                    one_hots(k, n)
                    split_u((k + 1) % 2, n * CHUNKS_A_TILE + k + 2)
                    if k == CHUNKS_A_TILE - 2:
                        M.ranking.rank_head(chain, n + 1, HEADS - 1)
                        M.ranking.name_head(chain, HEADS - 1)
                        shift()
                    elif k == CHUNKS_A_TILE - 1:
                        softmax(n + 2)
                    elif k % 2 == 0:
                        M.ranking.rank_head(chain, n + 1, k // 2)
                    else:
                        M.ranking.name_head(chain, k // 2)
                    add_lo(GROUPS_A_CHUNK * k, n)
                    if k == CHUNKS_A_TILE - 1:
                        picks_by_slot(n + 2)
                    add_lo(GROUPS_A_CHUNK * k + 1, n)
            chain.restart()
            for k in range(TS // (2 * GROUP)):
                one_hots(k, N_TILES)
                for g in range(GROUPS_A_CHUNK):
                    add_lo(GROUPS_A_CHUNK * k + g, N_TILES)


def combine(nc, io, M):
    with Phase(nc, "cb") as ph:
        raw = [ph.sb(f"raw{b}", [P, D]) for b in range(2)]
        v_hi = [ph.sb(f"vhi{b}", [P, SUPER, D], F32R) for b in range(2)]
        v_lo = [ph.sb(f"vlo{b}", [P, SUPER, D], F32R) for b in range(2)]
        c_hi = [ph.sb(f"chi{b}", [P, SUPER, T], F32R) for b in range(2)]
        c_lo = [ph.sb(f"clo{b}", [P, SUPER, T], F32R) for b in range(2)]
        wt = [ph.sb(f"wt{b}", [P, TH * SUPER]) for b in range(2)]
        hid = [ph.sb(f"hid{b}", [P, SUPER, TH]) for b in range(2)]
        bank = ph.ps("bank", [P, 8, 512])
        h_in = ph.sems("h_in", DC)
        v_in, v_round, v_split = ph.sems("v_in", 2), ph.sem("v_round"), ph.sem("v_split")
        c_in, c_made, c_round, c_split = ph.sems("c_in", 2), ph.sem("c_made"), ph.sem("c_round"), ph.sem("c_split")
        bank_done, added = ph.sem("bank_done"), ph.sem("added")
        squared, summed = ph.sem("squared"), ph.sem("summed")
        block = ph.block()
        v_rows = io["v_tab"][0].rearrange("(n p) d -> n p d", p=P)
        SUMS = DC * NTH
        supers = NKEYS // SUPER

        @block.sync
        def _(sp):
            start_free(sp, (v_split, v_split, c_split, c_split))
            with sp.Fori(0, supers // 2) as m:
                for b in range(2):
                    def load_third(th):
                        x = NTH * b + th
                        sp.wait_ge(c_split, 2 * NTH * m + x + 1)
                        sp.dma_start(wt[x % 2][:, :], M.weights[bass.ds(2 * m + b, 1), :, th * TH * SUPER:(th + 1) * TH * SUPER]
                                     .rearrange("a j t -> j (a t)")).then_inc(c_in[x % 2], 16)
                        sp.dma_start(hid[x % 2][:, :, :], M.hidden[bass.ds(2 * SUPER * m + SUPER * b, SUPER), :, th * TH:(th + 1) * TH]
                                     .rearrange("i j t -> j i t")).then_inc(c_in[x % 2], 16)

                    def load_v(i):
                        sp.wait_ge(v_split, 2 * SUPER * m + SUPER * b + i + 1)
                        sp.dma_start(raw[i % 2][:, :], v_rows[bass.ds(2 * SUPER * m + SUPER * b + i, 1), :, :]
                                     .rearrange("a p d -> p (a d)")).then_inc(v_in[i % 2], 16)

                    load_third(0)
                    load_v(0)
                    load_v(1)
                    load_third(1)
                    load_v(2)
                    load_third(2)
                    load_v(3)

        first = ("third", 0), ("v", 0), ("v", 1), ("third", 1), ("v", 2), ("third", 2), ("v", 3)

        @block.gpsimd
        def _(pool):
            def split_v(m, b):
                pool.wait_ge(bank_done, 2 * SUMS * m + SUMS * b + 1)
                for i in range(SUPER):
                    pool.wait_ge(v_in[i % 2], 16 * (SUPER * m + SUPER // 2 * b + i // 2 + 1))
                    pool.sem_inc(M.pool_passed, 1)
                    nc.gpsimd.tensor_copy(v_hi[b][:, i, :], raw[i % 2][:, :]).then_inc(v_round, 1)
                    pool.wait_ge(v_round, 2 * SUPER * m + SUPER * b + i + 1)
                    nc.gpsimd.tensor_tensor(v_lo[b][:, i, :], raw[i % 2][:, :], v_hi[b][:, i, :].bitcast(F32),
                                            ALU.subtract).then_inc(v_split, 1)

            pool.wait_ge(v_split, SUPER + 2)
            with pool.Fori(0, supers // 2 - 1) as m:
                split_v(m, 1)
                split_v(m + 1, 0)
            split_v(supers // 2 - 1, 1)

        @block.scalar
        def _(act):
            def round_third(m, b, th):
                x = NTH * b + th
                act.wait_ge(c_made, 2 * NTH * m + x + 1)
                nc.scalar.copy(c_hi[b][:, :, th * TH:(th + 1) * TH], hid[x % 2][:, :, :]).then_inc(c_round, 1)

            def round_coefficients(m, b):
                act.wait_ge(bank_done, 2 * SUMS * m + SUMS * b + 1)
                for th in range(NTH):
                    round_third(m, b, th)

            for kind, i in first:
                if kind == "third":
                    round_third(0, 0, i)
                else:
                    act.wait_ge(v_in[i % 2], 16 * (i // 2 + 1))
                    nc.scalar.copy(v_hi[0][:, i, :], raw[i % 2][:, :]).then_inc(v_round, 1)
                if i == 2 and kind == "v":
                    for c in range(DC):
                        act.dma_start(M.hT[:, c, :], M.h_spill[c]).then_inc(h_in[c], 16)
            with act.Fori(0, supers // 2 - 1) as m:
                round_coefficients(m, 1)
                round_coefficients(m + 1, 0)
            round_coefficients(supers // 2 - 1, 1)
            act.wait_ge(c_split, NTH * supers + 2)
            for c in range(DC):
                act.wait_ge(added, SUMS * (supers - 1) + NTH * (c + 1) + 8)
                if c >= 2:
                    act.wait_ge(summed, c - 1)
                nc.scalar.activation(flat(hid[c % 2][:, 0:NTH, :]), M.hT[:, c, :], ACT.Square).then_inc(squared, 1)

        @block.tensor
        def _(pe):
            pe.sem_inc(bank_done, SUMS + 1)
            pe.sem_inc(added, 8)
            with pe.Fori(0, supers // 2) as m:
                for b in range(2):
                    pe.wait_ge(v_split, 2 * SUPER * m + SUPER * (b + 1) + 2)
                    for r in range(SUMS):
                        mm, th = divmod(r, NTH)
                        if mm == 0:
                            pe.wait_ge(c_split, 2 * NTH * m + NTH * b + th + 1 + 2)
                        pe.wait_ge(added, 2 * SUMS * m + SUMS * b + r + 1)
                        ws, cols = slice(mm * P, (mm + 1) * P), slice(th * TH, (th + 1) * TH)
                        out = bank[:, r % 8, 0:TH]
                        for i in range(SUPER):
                            nc.tensor.matmul(out, v_hi[b][:, i, ws], c_hi[b][:, i, cols], start=(i == 0), stop=False)
                            nc.tensor.matmul(out, v_hi[b][:, i, ws], c_lo[b][:, i, cols], start=False, stop=False)
                            last = nc.tensor.matmul(out, v_lo[b][:, i, ws], c_hi[b][:, i, cols], start=False, stop=(i == SUPER - 1))
                        last.then_inc(bank_done, 1)

        @block.vector
        def _(dve):
            def make(m, x):
                dve.wait_ge(c_in[x % 2], 32 * (NTH * m + x // 2 + 1))
                nc.vector.tensor_tensor(hid[x % 2][:, :, :], hid[x % 2][:, :, :],
                                        wt[x % 2][:, :].rearrange("p (t i) -> p i t", i=SUPER), ALU.mult).then_inc(c_made, 1)

            def split(m, x):
                b, th = divmod(x, NTH)
                dve.wait_ge(c_round, 2 * NTH * m + x + 1)
                nc.vector.tensor_tensor(c_lo[b][:, :, th * TH:(th + 1) * TH], hid[x % 2][:, :, :],
                                        c_hi[b][:, :, th * TH:(th + 1) * TH].bitcast(F32), ALU.subtract).then_inc(c_split, 1)

            def add(m, b, r):
                mm, th = divmod(r, NTH)
                dve.wait_ge(bank_done, 2 * SUMS * m + SUMS * b + r + 1 + SUMS + 1)
                if b == 0 and th == 0:
                    dve.wait_ge(h_in[mm], 16)
                h = M.hT[:, mm, th * TH:(th + 1) * TH]
                nc.vector.tensor_tensor(h, h, bank[:, r % 8, 0:TH], ALU.add).then_inc(added, 1)

            def step(m, b, ahead):
                for r in range(SUMS):
                    th, odd = divmod(r, 6)
                    if th < NTH and odd == 0:
                        make(ahead, NTH * (1 - b) + th)
                    if th < NTH and odd == 4:
                        split(ahead, NTH * (1 - b) + th)
                    add(m, b, r)

            for kind, i in first:
                if kind == "third":
                    make(0, i)
                    split(0, i)
                else:
                    dve.wait_ge(v_round, i + 1)
                    nc.vector.tensor_tensor(v_lo[0][:, i, :], raw[i % 2][:, :], v_hi[0][:, i, :].bitcast(F32),
                                            ALU.subtract).then_inc(v_split, 1)
            with dve.Fori(0, supers // 2 - 1) as m:
                step(m, 0, m)
                step(m, 1, m + 1)
            step(supers // 2 - 1, 0, supers // 2 - 1)

            def sum_squares(c):
                dve.wait_ge(squared, c + 1)
                sq = flat(hid[c % 2][:, 0:NTH, :])
                if c == 0:
                    nc.vector.tensor_copy(M.total[:, :], sq).then_inc(summed, 1)
                else:
                    dve.wait_ge(summed, c)
                    nc.vector.tensor_tensor(M.total[:, :], M.total[:, :], sq, ALU.add).then_inc(summed, 1)

            for r in range(SUMS):
                add(supers // 2 - 1, 1, r)
                if r % NTH == NTH - 1 and r > NTH:
                    sum_squares(r // NTH - 1)
            sum_squares(DC - 1)


def layer_input_gate(nc, io, M, ws):
    with Phase(nc, "pg") as ph:
        KP = D_PLE // P
        p_rows = ph.sb("p_rows", [P, NT, D_PLE])
        pT = ph.sb("pT", [P, KP, T])
        wp = [ph.sb(f"wp{b}", [P, KP, P]) for b in range(2)]
        sig = [ph.sb(f"sig{b}", [P, T]) for b in range(2)]
        gate, proj = ph.ps("gate", [P, NTH, 512]), ph.ps("proj", [P, NTH, 512])
        turn = ph.ps("turn", [P, 2, 512])
        p_in, p_turned, p_out = ph.sem("p_in"), ph.sem("p_turned"), ph.sem("p_out")
        wp_in, proj_done, sigmoid, gated, added = ph.sems("wp_in", 2), ph.sem("proj_done"), ph.sem("sigmoid"), ph.sem("gated"), ph.sem("added")
        squares = SquareSum(nc, ph, M, sig)
        block = ph.block()
        wp_cols = io["w_ple_proj"][0].rearrange("(c p) e -> p c e", p=P)

        @block.sync
        def _(sp):
            sp.dma_start(p_rows[:, 0:N_TILES, :], io["p_prompt"][0, 0].rearrange("(n p) e -> p n e", p=P)).then_inc(p_in, 16)
            sp.dma_start(p_rows[0:TS, N_TILES, :], io["p_sample"][0].rearrange("b s e -> (b s) e")).then_inc(p_in, 16)
            start_free(sp, (proj_done, proj_done))

            def load_projection(n, b):
                sp.wait_ge(proj_done, 2 * n + b + 1)
                sp.dma_start(wp[b][:, :, :], wp_cols[:, :, bass.ds(2 * P * n + P * b, P)]).then_inc(wp_in[b], 16)

            for b in range(2):
                load_projection(0, b)
            with sp.Fori(1, ws.pairs) as n:
                for b in range(2):
                    ws.load(sp, n, b)
                    load_projection(n, b)

        @block.gpsimd
        def _(pool):
            squares.start(pool)
            ws.halve_rest(pool)

        @block.tensor
        def _(pe):
            pe.wait_ge(p_in, 32)
            for r in range(NT):
                if r >= 2:
                    pe.wait_ge(p_out, r - 1)
                rows = P if r < N_TILES else TS
                for k in range(KP):
                    last = nc.tensor.transpose(turn[:, r % 2, k * P:k * P + rows], p_rows[0:rows, r, k * P:(k + 1) * P],
                                               M.ident[0:rows, 0:rows])
                last.then_inc(p_turned, 1)
            pe.wait_ge(p_out, NT)
            start_free(pe, (sigmoid, gated))
            with pe.Fori(0, ws.pairs) as n:
                for b in range(2):
                    pe.wait_ge(sigmoid, 2 * n + b + 1)
                    ws.product(pe, n, b, gate, M.x_hi, M.x_lo)
                    pe.wait_ge(wp_in[b], 16 * n + 16)
                    pe.wait_ge(gated, 2 * n + b + 1)
                    for th in range(NTH):
                        for k in range(KP):
                            last = nc.tensor.matmul(proj[:, th, 0:TH], wp[b][:, k, :], pT[:, k, th * TH:(th + 1) * TH],
                                                    start=(k == 0), stop=(k == KP - 1))
                    last.then_inc(proj_done, 1)

        @block.scalar
        def _(act):
            for r in range(NT):
                act.wait_ge(p_turned, r + 1)
                rows = P if r < N_TILES else TS
                nc.scalar.copy(pT[:, :, r * P:r * P + rows],
                               turn[:, r % 2, 0:2 * P].rearrange("p (k t) -> p k t", k=KP)[:, :, 0:rows]).then_inc(p_out, 1)
            with act.Fori(0, ws.pairs) as n:
                for b in range(2):
                    act.wait_ge(ws.used[b], n + 2)
                    act.wait_ge(squares.summed, 2 * n + b + 1)
                    nc.scalar.activation(thirds(sig[b][:, :]), gate[:, :, 0:TH], ACT.Sigmoid).then_inc(sigmoid, 1)
                    act.wait_ge(added, 2 * n + b + 1)
                    squares.square(act, 2 * n + b, b)

        @block.vector
        def _(dve):
            with dve.Fori(0, ws.pairs) as n:
                for b in range(2):
                    dve.wait_ge(sigmoid, 2 * n + b + 2)
                    dve.wait_ge(proj_done, 2 * n + b + 3)
                    nc.vector.tensor_tensor(thirds(sig[b][:, :]), thirds(sig[b][:, :]), proj[:, :, 0:TH], ALU.mult).then_inc(gated, 1)
                    dve.wait_ge(gated, 2 * n + b + 2)
                    row = M.hT[:, bass.ds(2 * n + b, 1), :].rearrange("p o t -> p (o t)")
                    nc.vector.tensor_tensor(row, row, sig[b][:, :], ALU.add).then_inc(added, 1)
                    squares.add(dve, 2 * n + b, b)


def normalise_and_store(nc, io, M):
    with Phase(nc, "st") as ph:
        y = [ph.sb(f"y{b}", [P, D]) for b in range(2)]
        g_row = ph.sb("g_row", [P, D])
        std, rstd = ph.sb("std", [P, NT]), ph.sb("rstd", [P, NT])
        turn = [ph.ps(f"turn{b}", [P, DC, P]) for b in range(2)]
        mean = ph.ps("mean", [P, NT])
        g_in, summed, rooted, inverted = ph.sem("g_in"), ph.sem("summed"), ph.sem("rooted"), ph.sem("inverted")
        turned, scaled, stored = ph.sem("turned"), ph.sem("scaled"), ph.sems("stored", 2)
        block = ph.block()
        parts = ((P, slice(0, N_TILES)), (TS, slice(N_TILES, NT)))

        @block.tensor
        def _(pe):
            for t in range(NT):
                rows = P if t < N_TILES else TS
                last = nc.tensor.matmul(mean[0:rows, t:t + 1], M.total[:, t * P:t * P + rows], M.mean_d[:, 0:1],
                                        start=True, stop=True)
            last.then_inc(summed, 1)
            for t in range(NT):
                rows = P if t < N_TILES else TS
                if t >= 2:
                    pe.wait_ge(scaled, t - 1)
                for c in range(DC):
                    last = nc.tensor.transpose(turn[t % 2][0:rows, c, :], M.hT[:, c, t * P:t * P + rows], M.ident[:, :])
                last.then_inc(turned, 1)

        @block.scalar
        def _(act):
            act.dma_start(g_row[:, :], io["g_final"].partition_broadcast(P)).then_inc(g_in, 16)
            act.wait_ge(summed, 1)
            for rows, tiles in parts:
                nc.scalar.activation(std[0:rows, tiles], mean[0:rows, tiles], ACT.Sqrt, bias=M.eps[0:rows, 0:1]).then_inc(rooted, 1)

        @block.vector
        def _(dve):
            for k, (rows, tiles) in enumerate(parts):
                dve.wait_ge(rooted, k + 1)
                nc.vector.reciprocal(rstd[0:rows, tiles], std[0:rows, tiles]).then_inc(inverted, 1)
            dve.wait_ge(inverted, 2)
            dve.wait_ge(g_in, 16)
            for t in range(NT):
                rows = P if t < N_TILES else TS
                dve.wait_ge(turned, t + 1)
                if t >= 2:
                    dve.wait_ge(stored[t % 2], 16 * (t // 2))
                nc.vector.scalar_tensor_tensor(out=y[t % 2][0:rows, :], in0=flat(turn[t % 2][0:rows, :, :]),
                                               scalar=rstd[0:rows, t:t + 1], in1=g_row[0:rows, :],
                                               op0=ALU.mult, op1=ALU.mult).then_inc(scaled, 1)

        @block.sync
        def _(sp):
            for t in range(NT):
                sp.wait_ge(scaled, t + 1)
                if t < N_TILES:
                    sp.dma_start(io["y_prompt"][0, t * P:(t + 1) * P, :], y[t % 2][:, :]).then_inc(stored[t % 2], 16)
                else:
                    sp.dma_start(io["y_sample"].rearrange("b s d -> (b s) d"), y[t % 2][0:TS, :]).then_inc(stored[t % 2], 16)
            sp.wait_ge(stored[0], 16 * ((NT + 1) // 2))
            sp.wait_ge(stored[1], 16 * (NT // 2))


def clear_ended(nc, spared):
    ended = [s for s in ENDED if s not in spared]
    with nc.Block() as block:

        @block.sync
        def _(sp):
            for s in ended[0::3]:
                sp.sem_clear(s)

        @block.scalar
        def _(act):
            for s in ended[1::3]:
                act.sem_clear(s)

        @block.vector
        def _(dve):
            for s in ended[2::3]:
                dve.sem_clear(s)

    ENDED.clear()


class Memory:
    pass


def decoder_step(nc, io):
    ENDED.clear()
    with Phase(nc, "m") as ph:
        M = Memory()
        M.hidden = nc.dram_tensor("hidden", (NKEYS, P, T), F32).ap()
        M.weights = nc.dram_tensor("weights", (NKEYS // SUPER, P, T * SUPER), F32).ap()
        M.h_spill = nc.dram_tensor("h_spill", (DC, P, T), F32).ap()
        M.ident, M.iota = ph.sb("ident", [P, P]), ph.sb("iota", [P, P])
        M.mean_d, M.mean_c = ph.sb("mean_d", [P, P]), ph.sb("mean_c", [P, P])
        M.vec = ph.sb("vec", [P, NVEC])
        M.eps = ph.sb("eps", [P, 1])
        M.pool_passed, M.dve_passed = ph.sem("pool_passed"), ph.sem("dve_passed")
        with Phase(nc, "m1") as p1:
            M.x_hi, M.x_lo = p1.sb("x_hi", [P, DC, T], F32R), p1.sb("x_lo", [P, DC, T], F32R)
            with Phase(nc, "m2") as p2:
                M.hT = p2.sb("hT", [P, DC, T])
                M.mix = p2.sb("mix", [P, DC, T])
                M.taps = p2.sb("taps", [P, MC, TAPS + 1])
                M.pool_pre = p2.sb("pool_pre", [P, MC, DEC_B * POOL_PRE])
                M.conv_pre = p2.sb("conv_pre", [P, MC, DEC_B * CONV_PRE])
                M.plast = p2.sb("plast", [P, MC, POOL_PRE * (1 + DEC_B)])
                M.ulast = p2.sb("ulast", [P, MC, CONV_PRE * (1 + DEC_B)])
                with Phase(nc, "t1") as pt:
                    M.total = pt.sb("total", [P, T])
                    load_inputs(nc, io, M)
                    normalise(nc, M, "n1", VEC["g_mix"], M.x_hi, M.x_lo)
                mixer(nc, io, M)
                with Phase(nc, "t2") as pt:
                    M.total = pt.sb("total", [P, T])
                    ws = WeightStream(nc, pt, io["w_out"][0], DC)
                    mixer_tail(nc, io, M, ws)
                    out_projection(nc, M, ws)
                    normalise(nc, M, "n2", VEC["g_ffn"], M.x_hi, M.x_lo, spill=M.h_spill)
            with Phase(nc, "m3") as p3:
                M.sv, M.si = p3.sb("sv", [P, NT, 2 * HEADS, TOPK]), p3.sb("si", [P, NT, 2 * HEADS, TOPK])
                M.ranking = Ranking(nc, p3, M)
                key_scores(nc, io, M)
                hidden_and_weights(nc, io, M)
        with Phase(nc, "m4") as p4:
            M.hT, M.total = p4.sb("hT", [P, DC, T]), p4.sb("total", [P, T])
            clear_ended(nc, (M.pool_passed, M.dve_passed))
            combine(nc, io, M)
            with Phase(nc, "m5") as p5:
                M.x_hi, M.x_lo = p5.sb("x_hi", [P, DC, T], F32R), p5.sb("x_lo", [P, DC, T], F32R)
                ws = WeightStream(nc, p5, io["w_ple_gate"][0], DC)
                normalise(nc, M, "n3", VEC["g_ple"], M.x_hi, M.x_lo, ahead=ws)
                layer_input_gate(nc, io, M, ws)
            normalise_and_store(nc, io, M)




_OUTS = [("y_prompt", (1, SEQ, D)), ("y_sample", (DEC_B, DEC_S, D)),
         ("pool_state_prompt", (1, 1, POOL_PRE, D_HALF_MIX)), ("conv_state_prompt", (1, 1, CONV_PRE, D_HALF_MIX)),
         ("pool_state_sample", (1, DEC_B, POOL_PRE, D_HALF_MIX)), ("conv_state_sample", (1, DEC_B, CONV_PRE, D_HALF_MIX))]
_INS = ["x_prompt", "x_sample", "state_pool", "state_conv", "p_prompt", "p_sample", "g_mix", "w_in", "w_pool", "pool_scale",
        "w_dw", "b_dw", "ln_g", "ln_b", "w_out", "g_ffn", "w_q", "sub_keys", "u_tab", "v_tab", "g_ple", "w_ple_gate",
        "w_ple_proj", "g_final"]


def kernel(**inputs):
    import numpy as _np
    import concourse.bacc as _bacc
    from concourse import mybir as _mybir
    from concourse.bass_utils import run_bass_kernel_spmd as _run

    nc = _bacc.Bacc("TRN2", target_bir_lowering=False, num_devices=1)
    arrays, io = {}, {}
    for name in _INS:
        a = _np.ascontiguousarray(inputs[name])
        arrays[f"in_{name}_dram"] = a
        io[name] = nc.dram_tensor(f"in_{name}_dram", a.shape, _mybir.dt.from_np(a.dtype), kind="ExternalInput").ap()
    for name, shape in _OUTS:
        io[name] = nc.dram_tensor(f"out_{name}_dram", shape, _mybir.dt.float32, kind="ExternalOutput").ap()
    decoder_step(nc, io)
    r = _run(nc, [arrays], core_ids=[0])
    return tuple(r.results[0][f"out_{name}_dram"] for name, _ in _OUTS)
```
